# Optimizing a Trainium2 kernel written in Bass

```python
import math
import jax, jax.numpy as jnp
from jax import lax
import numpy as np

D_MODEL = 1024
BATCH = 1
SEQ = 256
DEPTH = 2

HEAD_DIM = 64
V_DIM = 2 * HEAD_DIM
ATTN_W = D_MODEL // 2
N_HEADS = ATTN_W // V_DIM
QK_W = N_HEADS * 2 * HEAD_DIM
CONV_W = D_MODEL // 2
CONV_K = 3
N_CONV_GROUPS = 8
D_FF = (((8 * D_MODEL) // 3 + 255) // 256) * 256
NUM_BUCKETS = 32
MAX_EXACT = NUM_BUCKETS // 2
MAX_DISTANCE = 128
Q_BLOCK = 128
NORM_EPS = 1e-6
SUBLN_EPS = 1e-5
COL_SIZES = (QK_W, QK_W, ATTN_W, CONV_W, CONV_W, CONV_W, D_MODEL, D_MODEL)
IN_COLS = sum(COL_SIZES)

kernel_name = "hybrid_diffattn_shortconv_macaron"

def rmsnorm(x, g, eps=NORM_EPS):
    xf = x.astype(jnp.float32)
    y = xf * lax.rsqrt(jnp.mean(xf * xf, axis=-1, keepdims=True) + eps)
    return (y * g.astype(jnp.float32)).astype(x.dtype)

def swiglu(h, w_gate, w_up, w_down):
    return (jax.nn.silu(h @ w_gate) * (h @ w_up)) @ w_down

def t5_causal_bucket(dist):
    n = jnp.maximum(dist, 0)
    is_small = n < MAX_EXACT
    nf = jnp.maximum(n, MAX_EXACT).astype(jnp.float32)
    large = MAX_EXACT + (jnp.log(nf / MAX_EXACT) / math.log(MAX_DISTANCE / MAX_EXACT)
                         * (NUM_BUCKETS - MAX_EXACT)).astype(jnp.int32)
    large = jnp.minimum(large, NUM_BUCKETS - 1)
    return jnp.where(is_small, n, large)

def diff_attention(q1, q2, k1, k2, v, rel_bias, lam):
    T = q1.shape[2]
    n_blocks = T // Q_BLOCK
    k_pos = jnp.arange(T, dtype=jnp.int32)

    def one_block(i):
        start = i * Q_BLOCK
        q1b = lax.dynamic_slice_in_dim(q1, start, Q_BLOCK, axis=2)
        q2b = lax.dynamic_slice_in_dim(q2, start, Q_BLOCK, axis=2)
        q_pos = start + jnp.arange(Q_BLOCK, dtype=jnp.int32)
        dist = q_pos[:, None] - k_pos[None, :]
        bias = jnp.transpose(rel_bias.astype(jnp.float32)[t5_causal_bucket(dist)], (2, 0, 1))
        visible = dist >= 0
        s1 = jnp.einsum('bhqd,bhkd->bhqk', q1b, k1).astype(jnp.float32) + bias
        s2 = jnp.einsum('bhqd,bhkd->bhqk', q2b, k2).astype(jnp.float32) + bias
        p1 = jax.nn.softmax(jnp.where(visible, s1, -jnp.inf), axis=-1)
        p2 = jax.nn.softmax(jnp.where(visible, s2, -jnp.inf), axis=-1)
        p = (p1 - lam * p2).astype(v.dtype)
        return jnp.einsum('bhqk,bhkd->bhqd', p, v)

    out = lax.map(one_block, jnp.arange(n_blocks, dtype=jnp.int32))
    nb, b, h, qb, dv = out.shape
    return jnp.transpose(out, (1, 0, 3, 2, 4)).reshape(b, nb * qb, h, dv)

def causal_depthwise_conv(u, w):
    c = u.shape[-1]
    return lax.conv_general_dilated(
        u, w[:, None, :].astype(u.dtype), window_strides=(1,), padding=[(CONV_K - 1, 0)],
        dimension_numbers=('NWC', 'WIO', 'NWC'), feature_group_count=c)

def setup_inputs(seed: int = 0) -> dict:
    key = jax.random.key(seed)
    ks = jax.random.split(key, 24)
    nrm = lambda k, shape, fan_in, s=1.0: jax.random.normal(k, shape, jnp.float32) * (s * fan_in ** -0.5)
    gain = lambda k, shape: 1.0 + 0.05 * jax.random.normal(k, shape, jnp.float32)
    return {
        "x": jax.random.normal(ks[0], (BATCH, SEQ, D_MODEL), jnp.float32),
        "norm_ffn1_g": gain(ks[1], (DEPTH, D_MODEL)),
        "ffn1_w_gate": nrm(ks[2], (DEPTH, D_MODEL, D_FF), D_MODEL),
        "ffn1_w_up": nrm(ks[3], (DEPTH, D_MODEL, D_FF), D_MODEL),
        "ffn1_w_down": nrm(ks[4], (DEPTH, D_FF, D_MODEL), D_FF),
        "norm_mix_g": gain(ks[5], (DEPTH, D_MODEL)),
        "w_in": nrm(ks[6], (DEPTH, D_MODEL, IN_COLS), D_MODEL),
        "lambda_q1": 0.1 * jax.random.normal(ks[7], (DEPTH, HEAD_DIM), jnp.float32),
        "lambda_k1": 0.1 * jax.random.normal(ks[8], (DEPTH, HEAD_DIM), jnp.float32),
        "lambda_q2": 0.1 * jax.random.normal(ks[9], (DEPTH, HEAD_DIM), jnp.float32),
        "lambda_k2": 0.1 * jax.random.normal(ks[10], (DEPTH, HEAD_DIM), jnp.float32),
        "subln_g": gain(ks[11], (DEPTH, V_DIM)),
        "rel_bias": 0.5 * jax.random.normal(ks[12], (NUM_BUCKETS, N_HEADS), jnp.float32),
        "conv_w": nrm(ks[13], (DEPTH, CONV_K, CONV_W), CONV_K),
        "w_branch_attn": nrm(ks[14], (DEPTH, ATTN_W, D_MODEL), ATTN_W),
        "w_branch_conv": nrm(ks[15], (DEPTH, CONV_W, D_MODEL), CONV_W),
        "w_out": nrm(ks[16], (DEPTH, D_MODEL, D_MODEL), D_MODEL),
        "norm_ffn2_g": gain(ks[17], (DEPTH, D_MODEL)),
        "ffn2_w_gate": nrm(ks[18], (DEPTH, D_MODEL, D_FF), D_MODEL),
        "ffn2_w_up": nrm(ks[19], (DEPTH, D_MODEL, D_FF), D_MODEL),
        "ffn2_w_down": nrm(ks[20], (DEPTH, D_FF, D_MODEL), D_FF),
        "final_g": gain(ks[21], (D_MODEL,)),
    }

def reference(x, norm_ffn1_g, ffn1_w_gate, ffn1_w_up, ffn1_w_down, norm_mix_g, w_in,
              lambda_q1, lambda_k1, lambda_q2, lambda_k2, subln_g, rel_bias, conv_w,
              w_branch_attn, w_branch_conv, w_out, norm_ffn2_g, ffn2_w_gate, ffn2_w_up,
              ffn2_w_down, final_g):
    B, T, _ = x.shape
    split_idx = list(np.cumsum(COL_SIZES)[:-1])
    q_scale = HEAD_DIM ** -0.5
    for l in range(DEPTH):
        lambda_init = 0.8 - 0.6 * math.exp(-0.3 * l)

        x = x + 0.5 * swiglu(rmsnorm(x, norm_ffn1_g[l]), ffn1_w_gate[l], ffn1_w_up[l], ffn1_w_down[l])

        h = rmsnorm(x, norm_mix_g[l])
        proj = h @ w_in[l]
        q, k, v, c_b, c_c, c_u, g_attn, g_conv = jnp.split(proj, split_idx, axis=-1)

        q = (q * q_scale).reshape(B, T, N_HEADS, 2, HEAD_DIM)
        k = k.reshape(B, T, N_HEADS, 2, HEAD_DIM)
        to_bhtd = lambda a: jnp.transpose(a, (0, 2, 1, 3))
        q1, q2 = to_bhtd(q[..., 0, :]), to_bhtd(q[..., 1, :])
        k1, k2 = to_bhtd(k[..., 0, :]), to_bhtd(k[..., 1, :])
        vh = to_bhtd(v.reshape(B, T, N_HEADS, V_DIM))
        lam = (jnp.exp(jnp.sum(lambda_q1[l].astype(jnp.float32) * lambda_k1[l].astype(jnp.float32)))
               - jnp.exp(jnp.sum(lambda_q2[l].astype(jnp.float32) * lambda_k2[l].astype(jnp.float32)))
               + lambda_init)
        attn = diff_attention(q1, q2, k1, k2, vh, rel_bias, lam)
        attn = rmsnorm(attn, subln_g[l], SUBLN_EPS) * (1.0 - lambda_init)
        y_attn = attn.reshape(B, T, ATTN_W) @ w_branch_attn[l]

        y_conv = (c_b * causal_depthwise_conv(c_c * c_u, conv_w[l])) @ w_branch_conv[l]

        merged = jax.nn.sigmoid(g_attn) * y_attn + jax.nn.sigmoid(g_conv) * y_conv
        x = x + merged @ w_out[l]

        x = x + 0.5 * swiglu(rmsnorm(x, norm_ffn2_g[l]), ffn2_w_gate[l], ffn2_w_up[l], ffn2_w_down[l])
    return rmsnorm(x, final_g)


_drawn_inputs = setup_inputs


def setup_inputs(seed=0):
    import zlib

    import numpy as np

    out = dict(_drawn_inputs(seed))
    spreads = {}
    factors = {'lambda_q2': 5.733}
    for name, (base, spread) in spreads.items():
        noise = np.random.default_rng([zlib.crc32(name.encode()), seed]).standard_normal(out[name].shape)
        drawn = base * np.exp(spread * noise) if base else spread * noise
        out[name] = __import__('jax').numpy.asarray(drawn.astype(out[name].dtype))
    for name, factor in factors.items():
        out[name] = (out[name] * factor).astype(out[name].dtype)
    return out
```

```python
import math
from contextlib import ExitStack, contextmanager

import numpy as np

import concourse.bass as bass
from concourse import mybir

F32 = mybir.dt.float32
F32R = mybir.dt.float32r
ACT = mybir.ActivationFunctionType
ALU = mybir.AluOpType
AX = mybir.AxisListType

P = 128
D_MODEL, SEQ, DEPTH = 1024, 256, 2
HEAD_DIM = 64
V_DIM = 2 * HEAD_DIM
ATTN_W = D_MODEL // 2
N_HEADS = ATTN_W // V_DIM
QK_W = N_HEADS * 2 * HEAD_DIM
CONV_W = D_MODEL // 2
CONV_K = 3
D_FF = (((8 * D_MODEL) // 3 + 255) // 256) * 256
NUM_BUCKETS = 32
MAX_EXACT = NUM_BUCKETS // 2
MAX_DISTANCE = 128
NORM_EPS = 1e-6
SUBLN_EPS = 1e-5
MASKED = -1.0e30

KT = D_MODEL // P
FT = D_FF // P
QT = SEQ // P
PAIR = 2
COLS = PAIR * P
UK = 4
RING = 4
LEAD = 2
ACCS = 2

COL_GATE_ATTN = 2 * QK_W + ATTN_W + 3 * CONV_W
COL_GATE_CONV = COL_GATE_ATTN + D_MODEL
COL_CONV_U = 2 * QK_W + ATTN_W + 2 * CONV_W

GU_ITERS = FT // PAIR
DOWN_UNITS = -(-FT // UK)
DOWN_ITERS = KT // PAIR // 2
QKV_ITERS = (2 * QK_W + ATTN_W) // (2 * COLS)
CONV_T = CONV_W // P
HEAD_ITERS = N_HEADS
UC_ITERS = 2
BRANCH_ITERS = KT // PAIR // 2
OUT_ITERS = KT // PAIR // 2

GU_UNITS, QKV_UNITS = 4, 4
DOWN_BODY = 2 * DOWN_UNITS
UNITS_LAYER = (2 * (GU_ITERS * GU_UNITS + DOWN_ITERS * DOWN_BODY)
               + 4 * (QKV_ITERS + HEAD_ITERS + UC_ITERS + 1 + BRANCH_ITERS + OUT_ITERS))
SETS_LAYER = 2 * 2 * (GU_ITERS + DOWN_ITERS) + 2 * (QKV_ITERS + HEAD_ITERS + UC_ITERS + 1) \
    + 4 * BRANCH_ITERS + 2 * OUT_ITERS
XPAIRS = KT // PAIR
NORMS_LAYER = 3
HEAD_STEPS = 7
STEPS_LAYER = 84

BIAS_ZERO = SEQ - 1
BIAS_LEN = SEQ + P
P_MIX, P_FFN2, P_NEXT, P_CONV, P_SUBLN, P_LAM = 0, KT, 2 * KT, 3 * KT, 3 * KT + CONV_K * CONV_T, \
    3 * KT + CONV_K * CONV_T + 1
PARS = P_LAM + 1


def lambda_init(layer):
    return 0.8 - 0.6 * math.exp(-0.3 * layer)


def bucket_places():
    n = np.arange(SEQ, dtype=np.int32)
    nf = np.maximum(n, MAX_EXACT).astype(np.float32)
    large = MAX_EXACT + (np.log(nf / np.float32(MAX_EXACT)) / np.float32(math.log(MAX_DISTANCE / MAX_EXACT))
                         * np.float32(NUM_BUCKETS - MAX_EXACT)).astype(np.int32)
    bucket = np.where(n < MAX_EXACT, n, np.minimum(large, NUM_BUCKETS - 1))
    places = np.zeros((NUM_BUCKETS, BIAS_LEN), np.float32)
    places[bucket, BIAS_ZERO - n] = 1.0
    return places


def at(t):
    return slice(t, t + PAIR) if isinstance(t, int) else bass.ds(t, PAIR)


class Count:

    def __init__(self, start=0):
        self.fixed, self.moving = start, 0

    def add(self, n=1):
        self.fixed += n
        return self.now

    @property
    def now(self):
        return self.moving + self.fixed


@contextmanager
def loop(eng, n, per):
    with eng.Fori(0, n) as i:
        before = {c: (c.fixed, c.moving) for c in per}
        for c, step in per.items():
            c.moving = c.moving + i * step
        yield i
        for c, step in per.items():
            fixed, moving = before[c]
            assert c.fixed - fixed == step, (c.fixed - fixed, step)
            c.fixed, c.moving = fixed + n * step, moving


def wait(eng, *pairs):
    for _, value in pairs:
        if not isinstance(value, int):
            eng.compute_val(value)
    for sem, value in pairs:
        eng.wait_ge(sem, value)


def trunk(nc, x, norm_ffn1_g, ffn1_w_gate, ffn1_w_up, ffn1_w_down, norm_mix_g, w_in,
          lambda_q1, lambda_k1, lambda_q2, lambda_k2, subln_g, rel_bias, conv_w,
          w_branch_attn, w_branch_conv, w_out, norm_ffn2_g, ffn2_w_gate, ffn2_w_up,
          ffn2_w_down, final_g, places, out):
    with ExitStack() as ctx:
        def sb(name, shape, dt=F32):
            return ctx.enter_context(nc.sbuf_tensor(name, [P, *shape], dt))

        def psum(name, shape):
            return ctx.enter_context(nc.psum_tensor(name, [P, *shape], F32))

        def sem(name):
            return ctx.enter_context(nc.semaphore(name))

        raw = sb("raw", [RING, UK, COLS])
        w_hi = sb("w_hi", [RING, UK, COLS], F32R)
        w_lo = sb("w_lo", [RING, UK, COLS], F32R)
        xt = sb("xt", [KT, SEQ])
        xg = sb("xg", [KT, SEQ])
        xm = sb("xm", [KT, 2 * SEQ], F32R)
        hm = sb("hm", [FT, 2 * SEQ], F32R)
        merged = hm[:, 0:KT, :]
        mix = hm[:, KT:2 * KT, :]
        proj = sb("proj", [3 * N_HEADS, SEQ])
        gates = sb("gates", [2 * KT, SEQ])
        x_tok = gates[:, 0:KT, :].rearrange("p k n -> p (k n)").rearrange("p (t d) -> p t d", t=QT)
        y_tok = gates[:, KT:2 * KT, :].rearrange("p k n -> p (k n)").rearrange("p (t d) -> p t d", t=QT)
        bias = sb("bias", [N_HEADS, SEQ + P])
        acc_lo = [sb(f"acc_lo{s}", [PAIR, SEQ]) for s in range(ACCS)]
        sums = [sb(f"sum{s}", [PAIR, SEQ]) for s in range(ACCS)]
        silu = sb("silu", [PAIR, SEQ])
        hid = sb("hid", [PAIR, SEQ])
        square = sb("square", [PAIR, SEQ])
        square_sum = sb("square_sum", [PAIR, SEQ])
        mean_sq = sb("mean_sq", [SEQ])
        root = sb("root", [SEQ])
        newton = sb("newton", [SEQ])
        inv = sb("inv", [SEQ])
        rstd = sb("rstd", [SEQ])
        half_rstd = sb("half_rstd", [SEQ])
        KEYS = SEQ + P
        head_qkv = sb("head_qkv", [3, SEQ])
        logits = sb("logits", [2, KEYS])
        expo = sb("expo", [2, KEYS])
        prob = sb("prob", [KEYS])
        row_max = sb("row_max", [QT, 2])
        neg_max = sb("neg_max", [QT, 2])
        row_sum = sb("row_sum", [QT, 2])
        row_inv = sb("row_inv", [QT, 2])
        lam_inv = sb("lam_inv", [QT])
        prob_t = sb("prob_t", [KEYS])
        v_tok = sb("v_tok", [QT, V_DIM])
        attn = sb("attn", [N_HEADS, QT, V_DIM])
        attn_ms = sb("attn_ms", [N_HEADS * QT])
        attn_root = sb("attn_root", [N_HEADS * QT])
        attn_newton = sb("attn_newton", [N_HEADS * QT])
        attn_inv = sb("attn_inv", [N_HEADS * QT])
        attn_rstd = sb("attn_rstd", [N_HEADS * QT])
        ident = sb("ident", [P])
        mean_ones = sb("mean_ones", [P])
        ones = sb("ones", [P])
        pars = sb("pars", [DEPTH, PARS])
        cur = sb("cur", [PARS])
        first_g = sb("first_g", [KT])
        lam_rows = sb("lam_rows", [4, DEPTH * HEAD_DIM])
        lam_prod = sb("lam_prod", [2, DEPTH * HEAD_DIM])
        lam_sum = sb("lam_sum", [2 * DEPTH])
        lam_exp = sb("lam_exp", [2, DEPTH])
        lam_diff = sb("lam_diff", [DEPTH])
        table = sb("table", [N_HEADS])
        table_wide = sb("table_wide", [N_HEADS, P])
        onehot = sb("onehot", [BIAS_LEN])
        bias_rows = gates[:, 0:2 * N_HEADS, :].rearrange("p k n -> p (k n)")[:, 0:N_HEADS * BIAS_LEN] \
            .rearrange("p (h m) -> p h m", h=N_HEADS)
        bias_dram = nc.dram_tensor("bias_scratch", (N_HEADS, P * BIAS_LEN), F32, kind="Internal").ap()

        acc = [psum(f"acc{s}", [PAIR, 2 * SEQ]) for s in range(ACCS)]
        score = psum("score", [2, 2 * SEQ])
        ps_c = psum("ps_c", [2 * SEQ])
        ps_d = psum("ps_d", [2 * SEQ])
        side = [score[:, 0, :], score[:, 1, :], ps_c[:, :], ps_d[:, :]]
        prob_t_ps = ps_c[:, 0:KEYS]
        v_ps = ps_d[:, 0:QT * V_DIM]
        pv_ps = ps_d[:, SEQ:SEQ + QT * V_DIM].rearrange("p (t d) -> p t d", t=QT)
        msq_ps = ps_c[:, 0:SEQ]

        loaded = [sem(f"loaded{s}") for s in range(RING)]
        x_loaded, pars_loaded, lam_loaded, table_loaded = (sem(n) for n in (
            "x_loaded", "pars_loaded", "lam_loaded", "table_loaded"))
        bias_stored, bias_loaded, out_stored = sem("bias_stored"), sem("bias_loaded"), sem("out_stored")
        hi_split = sem("hi_split")
        lo_split = sem("lo_split")
        used = sem("used")
        acc_copied = sem("acc_copied")
        acc_summed = sem("acc_summed")
        gate_ready, silu_done, hid_ready, hid_hi, hid_lo = (sem(n) for n in (
            "gate_ready", "silu_done", "hid_ready", "hid_hi", "hid_lo"))
        x_new, squared, square_added, xg_ready, xm_hi, xm_lo = (sem(n) for n in (
            "x_new", "squared", "square_added", "xg_ready", "xm_hi", "xm_lo"))
        msq_summed, msq_ready, root_ready = (sem(n) for n in ("msq_summed", "msq_ready", "root_ready"))
        scored, max_ready, exp_done, prob_ready, prob_turned, prob_copied = (sem(n) for n in (
            "scored", "max_ready", "exp_done", "prob_ready", "prob_turned", "prob_copied"))
        proj_ready, head_copied = sem("proj_ready"), sem("head_copied")
        v_turned, v_copied, pv_done, pv_read = (sem(n) for n in ("v_turned", "v_copied", "pv_done", "pv_read"))
        attn_ms_ready, attn_root_ready, attn_scaled, attn_turned, attn_gained, attn_hi = (sem(n) for n in (
            "attn_ms_ready", "attn_root_ready", "attn_scaled", "attn_turned", "attn_gained", "attn_hi"))
        mix_lo, conv_ready, conv_hi = sem("mix_lo"), sem("conv_ready"), sem("conv_hi")
        gates_done, merged_ready, merged_hi, merged_lo = (sem(n) for n in (
            "gates_done", "merged_ready", "merged_hi", "merged_lo"))
        vec_step, act_step = sem("vec_step"), sem("act_step")
        ident_zeroed, ident_ready, ones_ready = sem("ident_zeroed"), sem("ident_ready"), sem("ones_ready")
        x_turned, lam_summed, lam_spread, lam_exped = (sem(n) for n in (
            "x_turned", "lam_summed", "lam_spread", "lam_exped"))
        table_ready, bias_spread, bias_rows_ready = sem("table_ready"), sem("bias_spread"), sem("bias_rows_ready")
        y_ready, y_turned, y_copied = sem("y_ready"), sem("y_turned"), sem("y_copied")

        def wide(v):
            return v.unsqueeze(1).to_broadcast([P, PAIR, SEQ])

        block = ctx.enter_context(nc.Block())

        @block.sync
        def _(sp):
            split = Count(1)
            slot = [0]

            def load(src):
                s = slot[0] % RING
                sp.lower_ap_dma(src)
                wait(sp, (lo_split, split.now))
                sp.dma_start(raw[:, s, 0:src.shape[1], :], src).then_inc(loaded[s], 16)
                split.add()
                slot[0] += 1

            def rows(w, l):
                return w[bass.ds(l, 1)].rearrange("o (k p) n -> p (o k) n", p=P)

            def full(w, l, col):
                for k in range(0, KT, UK):
                    load(rows(w, l)[:, k:k + UK, bass.ds(col, COLS)])

            def down(w, l, col):
                for k in range(0, FT, UK):
                    load(rows(w, l)[:, k:min(k + UK, FT), bass.ds(col, COLS)])

            sp.dma_start(x_tok, x[0].rearrange("(t p) d -> p t d", p=P)).then_inc(x_loaded, 16)

            first = 0
            for k in range(0, KT, UK):
                load(rows(ffn1_w_gate, first)[:, k:k + UK, 0:COLS])
            with loop(sp, DEPTH, {split: UNITS_LAYER}) as l:
                with loop(sp, GU_ITERS - 1, {split: GU_UNITS}) as i:
                    full(ffn1_w_up, l, i * COLS)
                    full(ffn1_w_gate, l, i * COLS + COLS)
                full(ffn1_w_up, l, D_FF - COLS)
                with loop(sp, DOWN_ITERS, {split: DOWN_BODY}) as i:
                    for j in range(2):
                        down(ffn1_w_down, l, i * (2 * COLS) + j * COLS)
                with loop(sp, QKV_ITERS, {split: 4}) as i:
                    for j in range(2):
                        full(w_in, l, i * (2 * COLS) + j * COLS)
                with loop(sp, HEAD_ITERS, {split: 4}) as i:
                    full(w_in, l, i * COLS + COL_GATE_ATTN)
                    full(w_in, l, i * COLS + COL_GATE_CONV)
                with loop(sp, UC_ITERS, {split: 4}) as i:
                    for j in range(2):
                        full(w_in, l, COL_CONV_U + j * COLS - i * CONV_W)
                for j in range(2):
                    full(w_in, l, COL_CONV_U - 2 * CONV_W + j * COLS)
                with loop(sp, BRANCH_ITERS, {split: 4}) as i:
                    for j in range(2):
                        for w in (w_branch_attn, w_branch_conv):
                            load(rows(w, l)[:, :, bass.ds(i * (2 * COLS) + j * COLS, COLS)])
                with loop(sp, OUT_ITERS, {split: 4}) as i:
                    for j in range(2):
                        full(w_out, l, i * (2 * COLS) + j * COLS)
                with loop(sp, GU_ITERS, {split: GU_UNITS}) as i:
                    full(ffn2_w_gate, l, i * COLS)
                    full(ffn2_w_up, l, i * COLS)
                with loop(sp, DOWN_ITERS, {split: DOWN_BODY}) as i:
                    for j in range(2):
                        down(ffn2_w_down, l, i * (2 * COLS) + j * COLS)
                full(ffn1_w_gate, (l + 1) % DEPTH, 0)

            sp.wait_ge(y_copied, 4)
            sp.dma_start(out[0].rearrange("(t p) d -> p t d", p=P), y_tok).then_inc(out_stored, 16)
            sp.wait_ge(out_stored, 16)
            per_slot = (DEPTH * UNITS_LAYER + LEAD) // RING
            for s in range(RING):
                sp.wait_ge(loaded[s], 16 * (per_slot + (s < LEAD)))

        @block.gpsimd
        def _(pool):
            nc.gpsimd.memset(ident[:, :], 0.0).then_inc(ident_zeroed, 1)
            nc.gpsimd.memset(mean_ones[:, :], 1.0 / D_MODEL).then_inc(ones_ready, 1)
            nc.gpsimd.memset(ones[:, :], 1.0).then_inc(ones_ready, 1)
            pool.wait_ge(ident_zeroed, 1)
            nc.gpsimd.affine_select(out=ident[:, :], in_=ident[:, :], compare_op=ALU.not_equal, fill=1.0,
                                    base=0, pattern=[[-1, P]], channel_multiplier=1).then_inc(ident_ready, 1)
            pool.wait_ge(bias_rows_ready, 1)
            pool.dma_start(bias_dram.rearrange("h (p m) -> p h m", p=P), bias_rows).then_inc(bias_stored, 16)
            pool.wait_ge(bias_stored, 16)
            back = bias_dram[:, P - 1:P - 1 + P * (BIAS_LEN - 1)].rearrange("h (p m) -> p h m", p=P)
            pool.dma_start(bias[:, :, 0:SEQ], back[:, :, 0:SEQ]).then_inc(bias_loaded, 16)
            pool.dma_start(bias[:, :, SEQ:], back[:, :, P:SEQ]).then_inc(bias_loaded, 16)
            pool.wait_ge(bias_loaded, 32)

        @block.scalar
        def _(act):
            split = Count()
            loads = Count()
            sets = Count()
            pair = Count()
            norm = Count()
            hidden = Count()
            head = Count()
            projs = Count()
            layers = Count()
            branch_pairs = Count()
            spare = act.alloc_register("spare")
            slot = [0]
            units_done = Count(RING)

            def hi(tiles=UK):
                s = slot[0] % RING
                wait(act, (loaded[s], loads.now + 16), (used, split.now + 1))
                nc.scalar.copy(w_hi[:, s, 0:tiles, :], raw[:, s, 0:tiles, :]).then_inc(hi_split, 1)
                split.add()
                slot[0] += 1
                if slot[0] % RING == 0:
                    loads.add(16)

            def copy_acc(units):
                s = sets.fixed % ACCS
                units_done.add(units)
                wait(act, (used, units_done.now), (acc_summed, sets.now + 1))
                nc.scalar.copy(acc_lo[s][:, :, :], acc[s][:, :, SEQ:2 * SEQ]).then_inc(acc_copied, 1)
                sets.add()

            def moving_x(t, moving):
                pair.add()
                wait(act, (x_new, pair.now))
                if moving:
                    act.reg_mov(spare, 0)
                nc.scalar.activation(square[:, :, :], xt[:, at(t), :], ACT.Square).then_inc(squared, 1)
                wait(act, (xg_ready, pair.now))
                if moving:
                    act.reg_mov(spare, 0)
                nc.scalar.copy(xm[:, at(t), 0:SEQ], xg[:, at(t), :]).then_inc(xm_hi, 1)

            def norm_root():
                norm.add()
                wait(act, (msq_ready, norm.now))
                nc.scalar.activation(root[:, :], mean_sq[:, :], ACT.Sqrt).then_inc(root_ready, 1)

            def ffn():
                norm_root()
                with loop(act, GU_ITERS, {split: 4, loads: 16, sets: 2, units_done: 4, hidden: 1}) as i:
                    hi()
                    hi()
                    copy_acc(2)
                    hi()
                    hi()
                    hidden.add()
                    wait(act, (gate_ready, hidden.now))
                    nc.scalar.activation(silu[:, :, :], sums[0][:, :, :], ACT.Silu).then_inc(silu_done, 1)
                    copy_acc(2)
                    wait(act, (hid_ready, hidden.now))
                    act.reg_mov(spare, 0)
                    nc.scalar.copy(hm[:, bass.ds(i * PAIR, PAIR), 0:SEQ], hid[:, :, :]).then_inc(hid_hi, 1)
                with loop(act, DOWN_ITERS, {split: 12, loads: 48, sets: 2, units_done: 12, pair: 2}) as i:
                    for j in range(2):
                        for k in range(DOWN_UNITS):
                            u = k + LEAD
                            hi(FT - UK * (DOWN_UNITS - 1) if u == DOWN_UNITS - 1 else UK)
                        copy_acc(DOWN_UNITS)
                        moving_x(i * (2 * PAIR) + j * PAIR, True)

            def columns(v):
                return v.rearrange("(k p) -> p k", p=P)

            def par(l, at, src):
                act.dma_start(pars[:, l, at:at + src.shape[1]], src,
                              allow_slow_non_contiguous=True).then_inc(pars_loaded, 16)

            act.dma_start(first_g[:, :], columns(norm_ffn1_g[0]), allow_slow_non_contiguous=True) \
                .then_inc(pars_loaded, 16)
            for l in range(DEPTH):
                par(l, P_MIX, columns(norm_mix_g[l]))
                par(l, P_FFN2, columns(norm_ffn2_g[l]))
                par(l, P_NEXT, columns(norm_ffn1_g[l + 1] if l + 1 < DEPTH else final_g))
                par(l, P_SUBLN, columns(subln_g[l]))
                for k in range(CONV_K):
                    par(l, P_CONV + k * CONV_T, columns(conv_w[l, k]))
            for n, v in enumerate((lambda_q1, lambda_k1, lambda_q2, lambda_k2)):
                act.dma_start(lam_rows[0:1, n, :], v.rearrange("(o l) d -> o (l d)", o=1)).then_inc(lam_loaded, 16)
            act.dma_start(table[0:NUM_BUCKETS, :], rel_bias).then_inc(table_loaded, 16)
            act.dma_start(onehot[0:NUM_BUCKETS, :], places).then_inc(table_loaded, 16)
            for p in range(XPAIRS):
                moving_x(p * PAIR, False)
            wait(act, (lam_spread, 1))
            nc.scalar.activation(lam_exp[:, :, :], side[0][:, 0:2 * DEPTH].rearrange("p (s l) -> p s l", s=2),
                                 ACT.Exp).then_inc(lam_exped, 1)
            for _ in range(LEAD):
                hi()
            with loop(act, DEPTH, {split: UNITS_LAYER, loads: 4 * UNITS_LAYER, sets: SETS_LAYER,
                                   units_done: UNITS_LAYER, pair: 3 * XPAIRS, norm: NORMS_LAYER,
                                   hidden: 2 * GU_ITERS, head: N_HEADS, projs: 2 * QKV_ITERS, layers: 1,
                                   branch_pairs: XPAIRS}):
                ffn()
                norm_root()
                with loop(act, QKV_ITERS, {split: 4, loads: 16, sets: 2, units_done: 4}):
                    for _ in range(2):
                        hi()
                        hi()
                        copy_acc(2)
                projs.add(2 * QKV_ITERS)
                wait(act, (proj_ready, projs.now))
                with loop(act, HEAD_ITERS, {split: 4, loads: 16, sets: 2, units_done: 4, head: 1}) as h:
                    head.add()
                    nc.scalar.copy(head_qkv[:, :, :], proj[:, :, :].rearrange("p (a h) n -> p h a n", a=3)[
                        :, bass.ds(h, 1)].rearrange("p o a n -> p (o a) n")).then_inc(head_copied, 1)
                    hi()
                    hi()
                    wait(act, (v_turned, head.now))
                    nc.scalar.copy(v_tok[:, :, :].rearrange("p t d -> p (t d)"), v_ps).then_inc(v_copied, 1)
                    wait(act, (max_ready, head.now))
                    for t, (a, b) in enumerate(((SEQ, KEYS), (0, SEQ))):
                        for s in range(2):
                            last = nc.scalar.activation(expo[:, s, a:b], logits[:, s, a:b], ACT.Exp,
                                                        bias=neg_max[:, t, s:s + 1],
                                                        accum_out=row_sum[:, t, s:s + 1])
                    last.then_inc(exp_done, 1)
                    copy_acc(2)
                    hi()
                    hi()
                    wait(act, (prob_turned, head.now))
                    nc.scalar.copy(prob_t[:, :], prob_t_ps).then_inc(prob_copied, 1)
                    copy_acc(2)
                    wait(act, (pv_done, head.now))
                    act.reg_mov(spare, 0)
                    nc.scalar.copy(attn[:, bass.ds(h, 1)].rearrange("p o t d -> p (o t) d"),
                                   pv_ps).then_inc(pv_read, 1)
                with loop(act, UC_ITERS, {split: 4, loads: 16, sets: 2, units_done: 4}):
                    for _ in range(2):
                        hi()
                        hi()
                        copy_acc(2)
                layers.add()
                hi()
                hi()
                wait(act, (attn_ms_ready, layers.now))
                nc.scalar.activation(attn_root[:, :], attn_ms[:, :], ACT.Sqrt).then_inc(attn_root_ready, 1)
                copy_acc(2)
                wait(act, (attn_turned, layers.now))
                for b in range(2):
                    last = nc.scalar.activation(
                        attn[:, 2 * b:2 * b + 2].rearrange("p h t d -> p (h t d)"), side[b], ACT.Copy,
                        scale=cur[:, P_SUBLN:P_SUBLN + 1])
                last.then_inc(attn_gained, 1)
                wait(act, (attn_gained, layers.now))
                nc.scalar.copy(mix[:, 0:N_HEADS, 0:SEQ],
                               attn[:, :, :, :].rearrange("p h t d -> p h (t d)")).then_inc(attn_hi, 1)
                hi()
                hi()
                copy_acc(2)
                wait(act, (conv_ready, layers.now))
                nc.scalar.copy(mix[:, N_HEADS:, 0:SEQ], proj[:, 2 * CONV_T:3 * CONV_T, :]).then_inc(conv_hi, 1)
                with loop(act, BRANCH_ITERS, {split: 4, loads: 16, sets: 4, units_done: 4, branch_pairs: 2}) as i:
                    for j in range(2):
                        hi()
                        hi()
                        branch_pairs.add()
                        for g in range(2):
                            g_at = gates[:, bass.ds(i * (2 * PAIR) + g * KT + j * PAIR, PAIR), :]
                            last = nc.scalar.activation(g_at, g_at, ACT.Sigmoid)
                        last.then_inc(gates_done, 1)
                        copy_acc(1)
                        copy_acc(1)
                        wait(act, (merged_ready, branch_pairs.now))
                        act.reg_mov(spare, 0)
                        nc.scalar.copy(merged[:, bass.ds(i * (2 * PAIR) + j * PAIR, PAIR), 0:SEQ],
                                       hid[:, :, :]).then_inc(merged_hi, 1)
                with loop(act, OUT_ITERS, {split: 4, loads: 16, sets: 2, units_done: 4, pair: 2}) as i:
                    for j in range(2):
                        hi()
                        hi()
                        copy_acc(2)
                        moving_x(i * (2 * PAIR) + j * PAIR, True)
                ffn()
            norm_root()
            for b in range(4):
                act.wait_ge(y_turned, b + 1)
                nc.scalar.copy(y_tok[:, :, 2 * b * P:(2 * b + 2) * P].rearrange("p t (k d) -> p k t d", k=2),
                               side[b].rearrange("p (k t d) -> p k t d", k=2, t=QT)).then_inc(y_copied, 1)

        @block.vector
        def _(dve):
            split = Count()
            sets = Count()
            pair = Count()
            norm = Count()
            hidden = Count()
            head = Count()
            layers = Count()
            branch_pairs = Count()
            step = Count()
            slot = [0]

            def own(ins):
                ins.then_inc(vec_step, 1)
                step.add()
                wait(dve, (vec_step, step.now))

            def lo(tiles=UK):
                s = slot[0] % RING
                wait(dve, (hi_split, split.now + 1))
                nc.vector.tensor_tensor(w_lo[:, s, 0:tiles, :], raw[:, s, 0:tiles, :], w_hi[:, s, 0:tiles, :],
                                        ALU.subtract).then_inc(lo_split, 1)
                split.add()
                slot[0] += 1

            def sum_acc():
                s = sets.fixed % ACCS
                sets.add()
                wait(dve, (acc_copied, sets.now))
                nc.vector.tensor_tensor(sums[s][:, :, :], acc[s][:, :, 0:SEQ], acc_lo[s][:, :, :],
                                        ALU.add).then_inc(acc_summed, 1)
                wait(dve, (acc_summed, sets.now + ACCS))
                return sums[s][:, :, :]

            def moving_x(t, gains):
                pair.add()
                x_at, g_at, m_at = (v[:, at(t), :] for v in (xt, xg, xm))
                gain = gains.unsqueeze(2).to_broadcast([P, PAIR, SEQ])
                for ap in (x_at, g_at, gain, m_at[:, :, 0:SEQ], m_at[:, :, SEQ:2 * SEQ]):
                    dve.lower_ap(ap)
                wait(dve, (x_new, pair.now))
                nc.vector.tensor_tensor(g_at, x_at, gain, ALU.mult).then_inc(xg_ready, 1)
                wait(dve, (squared, pair.now))
                nc.vector.tensor_tensor(square_sum[:, :, :], square_sum[:, :, :], square[:, :, :],
                                        ALU.add).then_inc(square_added, 1)
                wait(dve, (xm_hi, pair.now))
                nc.vector.tensor_tensor(m_at[:, :, SEQ:2 * SEQ], g_at, m_at[:, :, 0:SEQ],
                                        ALU.subtract).then_inc(xm_lo, 1)

            def norm_rstd():
                norm.add()
                wait(dve, (msq_summed, norm.now))
                nc.vector.memset(square_sum[:, :, :], 0.0)
                nc.vector.tensor_scalar(mean_sq[:, :], msq_ps, NORM_EPS, None, ALU.add).then_inc(msq_ready, 1)
                wait(dve, (root_ready, norm.now))
                own(nc.vector.reciprocal(inv[:, :], root[:, :]))
                own(nc.vector.tensor_tensor(newton[:, :], inv[:, :], inv[:, :], ALU.mult))
                own(nc.vector.tensor_tensor(newton[:, :], newton[:, :], mean_sq[:, :], ALU.mult))
                own(nc.vector.tensor_scalar(newton[:, :], newton[:, :], -0.5, 1.5, ALU.mult, ALU.add))
                own(nc.vector.tensor_tensor(rstd[:, :], inv[:, :], newton[:, :], ALU.mult))
                nc.vector.tensor_scalar(half_rstd[:, :], rstd[:, :], 0.5, None, ALU.mult)

            def ffn(g_next):
                norm_rstd()
                with loop(dve, GU_ITERS, {split: 4, sets: 2, hidden: 1, step: 0}) as i:
                    lo()
                    lo()
                    summed = sum_acc()
                    nc.vector.tensor_tensor(summed, summed, wide(rstd[:, :]),
                                            ALU.mult).then_inc(gate_ready, 1)
                    lo()
                    lo()
                    hidden.add()
                    up = sum_acc()
                    wait(dve, (silu_done, hidden.now))
                    nc.vector.tensor_tensor(hid[:, :, :], up, silu[:, :, :],
                                            ALU.mult).then_inc(hid_ready, 1)
                    h_at = hm[:, bass.ds(i * PAIR, PAIR), :]
                    for ap in (h_at[:, :, 0:SEQ], h_at[:, :, SEQ:2 * SEQ]):
                        dve.lower_ap(ap)
                    wait(dve, (hid_hi, hidden.now))
                    nc.vector.tensor_tensor(h_at[:, :, SEQ:2 * SEQ], hid[:, :, :], h_at[:, :, 0:SEQ],
                                            ALU.subtract).then_inc(hid_lo, 1)
                with loop(dve, DOWN_ITERS, {split: 12, sets: 2, pair: 2, step: 2}) as i:
                    for j in range(2):
                        for k in range(DOWN_UNITS):
                            u = k + LEAD
                            lo(FT - UK * (DOWN_UNITS - 1) if u == DOWN_UNITS - 1 else UK)
                        t = i * (2 * PAIR) + j * PAIR
                        x_at = xt[:, at(t), :]
                        dve.lower_ap(x_at)
                        summed = sum_acc()
                        own(nc.vector.tensor_tensor(summed, summed, wide(half_rstd[:, :]),
                                                    ALU.mult))
                        nc.vector.tensor_tensor(x_at, x_at, summed, ALU.add).then_inc(x_new, 1)
                        moving_x(t, cur[:, bass.ds(i * (2 * PAIR) + (g_next + j * PAIR), PAIR)])

            dve.sem_inc(used, RING)
            dve.sem_inc(lo_split, RING)
            dve.sem_inc(acc_summed, ACCS)
            dve.sem_inc(pv_read, 1)
            nc.vector.memset(square_sum[:, :, :], 0.0)
            dve.wait_ge(pars_loaded, 16 * (1 + DEPTH * (4 + CONV_K)))
            for p in range(XPAIRS):
                dve.wait_ge(x_turned, p + 1)
                nc.vector.tensor_copy(xt[:, 2 * p:2 * p + 2, :].rearrange("p k n -> p (k n)"),
                                      side[p]).then_inc(x_new, 1)
                moving_x(p * PAIR, first_g[:, p * PAIR:(p + 1) * PAIR])
            dve.wait_ge(lam_loaded, 64)
            for s in range(2):
                last = nc.vector.tensor_tensor(lam_prod[0:1, s, :], lam_rows[0:1, 2 * s, :],
                                               lam_rows[0:1, 2 * s + 1, :], ALU.mult)
            own(last)
            nc.vector.tensor_reduce(
                lam_sum[0:1, :], lam_prod[0:1, :, :].rearrange("p s (l d) -> p (s l) d", l=DEPTH),
                AX.X, ALU.add).then_inc(lam_summed, 1)
            dve.wait_ge(table_loaded, 32)
            nc.vector.tensor_copy(
                table_wide[0:NUM_BUCKETS, :, :],
                table[0:NUM_BUCKETS, :].unsqueeze(2).to_broadcast([NUM_BUCKETS, N_HEADS, P])
            ).then_inc(table_ready, 1)
            dve.wait_ge(lam_exped, 1)
            own(nc.vector.tensor_tensor(lam_diff[:, :], lam_exp[:, 0, :], lam_exp[:, 1, :], ALU.subtract))
            for l in range(DEPTH):
                nc.vector.tensor_scalar(pars[:, l, P_LAM:P_LAM + 1], lam_diff[:, l:l + 1], lambda_init(l),
                                        None, ALU.add)
                own(nc.vector.tensor_scalar(pars[:, l, P_SUBLN:P_SUBLN + 1], pars[:, l, P_SUBLN:P_SUBLN + 1],
                                            1.0 - lambda_init(l), None, ALU.mult))
            dve.wait_ge(bias_spread, 1)
            for h in range(N_HEADS):
                last = nc.vector.tensor_copy(bias_rows[:, h, :], side[h][:, 0:BIAS_LEN])
            own(last)
            nc.vector.memset(bias_rows[:, :, BIAS_ZERO + 1:], MASKED).then_inc(bias_rows_ready, 1)
            for _ in range(LEAD):
                lo()
            with loop(dve, DEPTH, {split: UNITS_LAYER, sets: SETS_LAYER, pair: 3 * XPAIRS, norm: NORMS_LAYER,
                                   hidden: 2 * GU_ITERS, head: N_HEADS, layers: 1, branch_pairs: XPAIRS,
                                   step: STEPS_LAYER}) as l:
                par_at = pars[:, bass.ds(l, 1), :].rearrange("p o n -> p (o n)")
                own(nc.vector.tensor_copy(cur[:, :], par_at))
                ffn(P_MIX)
                norm_rstd()
                with loop(dve, QKV_ITERS, {split: 4, sets: 2}) as i:
                    for j in range(2):
                        lo()
                        lo()
                        p_at = proj[:, bass.ds(i * (2 * PAIR) + j * PAIR, PAIR), :]
                        dve.lower_ap(p_at)
                        summed = sum_acc()
                        nc.vector.tensor_tensor(p_at, summed, wide(rstd[:, :]), ALU.mult) \
                            .then_inc(proj_ready, 1)
                dve.wait_ge(bias_loaded, 32)
                with loop(dve, HEAD_ITERS, {split: 4, sets: 2, head: 1, step: HEAD_STEPS}) as h:
                    head.add()
                    lo()
                    lo()
                    b_at = bias[:, bass.ds(h, 1), :].to_broadcast([P, 2, KEYS])
                    dve.lower_ap(b_at)
                    wait(dve, (scored, head.now))
                    own(nc.vector.scalar_tensor_tensor(out=logits[:, :, :], in0=score[:, :, 0:KEYS],
                                                       scalar=HEAD_DIM ** -0.5, in1=b_at, op0=ALU.mult,
                                                       op1=ALU.add))
                    nc.vector.tensor_reduce(row_max[:, 1, :], logits[:, :, 0:SEQ], AX.X, ALU.max)
                    own(nc.vector.tensor_reduce(row_max[:, 0, :], logits[:, :, SEQ:], AX.X, ALU.max))
                    nc.vector.tensor_scalar(neg_max[:, :, :], row_max[:, :, :], -1.0, None,
                                            ALU.mult).then_inc(max_ready, 1)
                    g_at = gates[:, bass.ds(h * PAIR, PAIR), :]
                    dve.lower_ap(g_at)
                    summed = sum_acc()
                    own(nc.vector.tensor_tensor(g_at, summed, wide(rstd[:, :]), ALU.mult))
                    wait(dve, (exp_done, head.now))
                    own(nc.vector.reciprocal(row_inv[:, :, :], row_sum[:, :, :]))
                    own(nc.vector.tensor_scalar(lam_inv[:, :], row_inv[:, :, 1], cur[:, P_LAM:P_LAM + 1], None,
                                                ALU.mult))
                    for t, (a, b) in enumerate(((SEQ, KEYS), (0, SEQ))):
                        own(nc.vector.tensor_scalar(expo[:, 1, a:b], expo[:, 1, a:b], lam_inv[:, t:t + 1], None,
                                                    ALU.mult))
                        last = nc.vector.scalar_tensor_tensor(
                            out=prob[:, a:b], in0=expo[:, 0, a:b], scalar=row_inv[:, t, 0:1], in1=expo[:, 1, a:b],
                            op0=ALU.mult, op1=ALU.subtract)
                    last.then_inc(prob_ready, 1)
                    lo()
                    lo()
                    g_at = gates[:, bass.ds(h * PAIR + KT, PAIR), :]
                    dve.lower_ap(g_at)
                    summed = sum_acc()
                    nc.vector.tensor_tensor(g_at, summed, wide(rstd[:, :]), ALU.mult)
                with loop(dve, UC_ITERS, {split: 4, sets: 2}) as i:
                    for j in range(2):
                        lo()
                        lo()
                        p_at = proj[:, bass.ds(i * (2 * PAIR) + j * PAIR, PAIR), :]
                        dve.lower_ap(p_at)
                        summed = sum_acc()
                        nc.vector.tensor_tensor(p_at, summed, wide(rstd[:, :]), ALU.mult)
                layers.add()
                rows_at = attn[:, :, :, :].rearrange("p h t d -> p (h t) d")
                rows_sq = xg[:, 0:N_HEADS, :].rearrange("p h (t d) -> p (h t) d", t=QT)
                wait(dve, (pv_read, head.now + 1))
                own(nc.vector.tensor_tensor(rows_sq, rows_at, rows_at, ALU.mult))
                own(nc.vector.tensor_reduce(attn_ms[:, :], rows_sq, AX.X, ALU.add))
                own(nc.vector.tensor_scalar(attn_ms[:, :], attn_ms[:, :], 1.0 / V_DIM, SUBLN_EPS,
                                            ALU.mult, ALU.add))
                nc.vector.tensor_copy(attn_newton[:, :], attn_ms[:, :]).then_inc(attn_ms_ready, 1)
                lo()
                lo()
                wait(dve, (attn_root_ready, layers.now))
                own(nc.vector.reciprocal(attn_inv[:, :], attn_root[:, :]))
                own(nc.vector.tensor_tensor(attn_newton[:, :], attn_inv[:, :], attn_inv[:, :], ALU.mult))
                own(nc.vector.tensor_tensor(attn_newton[:, :], attn_newton[:, :], attn_ms[:, :], ALU.mult))
                own(nc.vector.tensor_scalar(attn_newton[:, :], attn_newton[:, :], -0.5, 1.5, ALU.mult, ALU.add))
                own(nc.vector.tensor_tensor(attn_rstd[:, :], attn_inv[:, :], attn_newton[:, :], ALU.mult))
                nc.vector.tensor_tensor(rows_at, rows_at,
                                        attn_rstd[:, :].unsqueeze(2).to_broadcast([P, N_HEADS * QT, V_DIM]),
                                        ALU.mult).then_inc(attn_scaled, 1)
                own(nc.vector.tensor_tensor(proj[:, 0:CONV_T, :], proj[:, 0:CONV_T, :],
                                            proj[:, CONV_T:2 * CONV_T, :], ALU.mult))
                for t in range(CONV_T):
                    u, y = proj[:, t, :], proj[:, CONV_T + t, :]
                    taps = [cur[:, P_CONV + k * CONV_T + t:P_CONV + k * CONV_T + t + 1] for k in range(CONV_K)]
                    own(nc.vector.tensor_scalar(y, u, taps[CONV_K - 1], None, ALU.mult))
                    for d in range(1, CONV_K):
                        own(nc.vector.scalar_tensor_tensor(
                            out=y[:, d:], in0=u[:, 0:SEQ - d], scalar=taps[CONV_K - 1 - d], in1=y[:, d:],
                            op0=ALU.mult, op1=ALU.add))
                summed = sum_acc()
                b_at = proj[:, 2 * CONV_T:2 * CONV_T + PAIR, :]
                own(nc.vector.tensor_tensor(b_at, summed, wide(rstd[:, :]), ALU.mult))
                own(nc.vector.tensor_tensor(b_at, b_at, proj[:, CONV_T:CONV_T + PAIR, :], ALU.mult))
                lo()
                lo()
                wait(dve, (attn_hi, layers.now))
                nc.vector.tensor_tensor(mix[:, 0:N_HEADS, SEQ:2 * SEQ],
                                        attn[:, :, :, :].rearrange("p h t d -> p h (t d)"),
                                        mix[:, 0:N_HEADS, 0:SEQ], ALU.subtract).then_inc(mix_lo, 1)
                summed = sum_acc()
                b_at = proj[:, 2 * CONV_T + PAIR:2 * CONV_T + 2 * PAIR, :]
                own(nc.vector.tensor_tensor(b_at, summed, wide(rstd[:, :]), ALU.mult))
                nc.vector.tensor_tensor(b_at, b_at, proj[:, CONV_T + PAIR:2 * CONV_T, :],
                                        ALU.mult).then_inc(conv_ready, 1)
                wait(dve, (conv_hi, layers.now))
                nc.vector.tensor_tensor(mix[:, N_HEADS:, SEQ:2 * SEQ], proj[:, 2 * CONV_T:3 * CONV_T, :],
                                        mix[:, N_HEADS:, 0:SEQ], ALU.subtract).then_inc(mix_lo, 1)
                with loop(dve, BRANCH_ITERS, {split: 4, sets: 4, branch_pairs: 2, step: 4}) as i:
                    for j in range(2):
                        lo()
                        lo()
                        branch_pairs.add()
                        t = i * (2 * PAIR) + j * PAIR
                        ga, gc = (gates[:, bass.ds(t + g * KT, PAIR), :] for g in range(2))
                        m_at = merged[:, at(t), :]
                        for ap in (ga, gc, m_at[:, :, 0:SEQ], m_at[:, :, SEQ:2 * SEQ]):
                            dve.lower_ap(ap)
                        summed = sum_acc()
                        wait(dve, (gates_done, branch_pairs.now))
                        own(nc.vector.tensor_tensor(summed, summed, ga, ALU.mult))
                        up = sum_acc()
                        own(nc.vector.tensor_tensor(up, up, gc, ALU.mult))
                        nc.vector.tensor_tensor(hid[:, :, :], summed, up,
                                                ALU.add).then_inc(merged_ready, 1)
                        wait(dve, (merged_hi, branch_pairs.now))
                        nc.vector.tensor_tensor(m_at[:, :, SEQ:2 * SEQ], hid[:, :, :], m_at[:, :, 0:SEQ],
                                                ALU.subtract).then_inc(merged_lo, 1)
                with loop(dve, OUT_ITERS, {split: 4, sets: 2, pair: 2}) as i:
                    for j in range(2):
                        lo()
                        lo()
                        t = i * (2 * PAIR) + j * PAIR
                        x_at = xt[:, at(t), :]
                        dve.lower_ap(x_at)
                        summed = sum_acc()
                        nc.vector.tensor_tensor(x_at, x_at, summed, ALU.add).then_inc(x_new, 1)
                        moving_x(t, cur[:, bass.ds(i * (2 * PAIR) + (P_FFN2 + j * PAIR), PAIR)])
                ffn(P_NEXT)
            norm_rstd()
            nc.vector.tensor_tensor(xg[:, :, :], xg[:, :, :], rstd[:, :].unsqueeze(1).to_broadcast([P, KT, SEQ]),
                                    ALU.mult).then_inc(y_ready, 1)

        @block.tensor
        def _(pe):
            unit = Count()
            sets = Count()
            norm = Count()
            pairs = Count()
            hidden = Count()
            head = Count()
            layers = Count()
            mixes = Count()
            branch_pairs = Count()
            slot = [0]

            def multiply(s, x_tiles, first, last, *needs):
                r = slot[0] % RING
                wait(pe, *needs, (hi_split, unit.now + 1), (lo_split, unit.now + 1 + RING))
                for k, x in enumerate(x_tiles):
                    for m in range(PAIR):
                        cols = slice(m * P, (m + 1) * P)
                        end = last and k == len(x_tiles) - 1
                        nc.tensor.matmul(acc[s][:, m, :], w_hi[:, r, k, cols], x[:, 0:2 * SEQ],
                                         start=first and k == 0, stop=False, skip_group_check=True)
                        mm = nc.tensor.matmul(acc[s][:, m, 0:SEQ], w_lo[:, r, k, cols], x[:, 0:SEQ],
                                              start=False, stop=end, skip_group_check=True)
                mm.then_inc(used, 1)
                unit.add()
                slot[0] += 1

            def new_set():
                s = sets.fixed % ACCS
                sets.add()
                wait(pe, (acc_summed, sets.now))
                return s

            def project(tiles, made, count):
                s = new_set()
                for n in range(KT // UK):
                    missing = (KT // UK - 1 - n) * UK // PAIR
                    multiply(s, [tiles[:, n * UK + k, :] for k in range(UK)], n == 0, n == KT // UK - 1,
                             (made, count.now - missing))

            def mean_square():
                wait(pe, (square_added, pairs.now))
                for m in range(PAIR):
                    mm = nc.tensor.matmul(msq_ps, mean_ones[:, :], square_sum[:, m, :], start=(m == 0),
                                          stop=(m == PAIR - 1))
                mm.then_inc(msq_summed, 1)
                norm.add()

            def ffn():
                mean_square()
                with loop(pe, GU_ITERS, {unit: 4, sets: 2}):
                    project(xm, xm_lo, pairs)
                    project(xm, xm_lo, pairs)
                hidden.add(GU_ITERS)
                with loop(pe, DOWN_ITERS, {unit: 12, sets: 2}):
                    for _ in range(2):
                        s = new_set()
                        for n in range(DOWN_UNITS):
                            tiles = range(n * UK, min((n + 1) * UK, FT))
                            multiply(s, [hm[:, k, :] for k in tiles], n == 0, n == DOWN_UNITS - 1,
                                     (hid_lo, hidden.now - (FT - 1 - tiles[-1]) // PAIR))
                pairs.add(XPAIRS)

            pe.wait_ge(ident_ready, 1)
            pe.wait_ge(x_loaded, 16)
            for b in range(4):
                for k in range(2):
                    for t in range(QT):
                        col = (k * QT + t) * P
                        kt = 2 * b + k
                        mm = nc.tensor.transpose(side[b][:, col:col + P], x_tok[:, t, kt * P:(kt + 1) * P],
                                                 ident[:, :])
                mm.then_inc(x_turned, 1)
            pairs.add(XPAIRS)
            pe.wait_ge(ones_ready, 2)
            pe.wait_ge(x_new, XPAIRS)
            pe.wait_ge(lam_summed, 1)
            nc.tensor.matmul(side[0][:, 0:2 * DEPTH], ones[0:1, :], lam_sum[0:1, :], start=True,
                             stop=True).then_inc(lam_spread, 1)
            pe.wait_ge(lam_exped, 1)
            pe.wait_ge(table_ready, 1)
            for h in range(N_HEADS):
                mm = nc.tensor.matmul(side[h][:, 0:BIAS_LEN], table_wide[0:NUM_BUCKETS, h, :],
                                      onehot[0:NUM_BUCKETS, :], start=True, stop=True)
            mm.then_inc(bias_spread, 1)
            pe.wait_ge(bias_rows_ready, 1)
            with loop(pe, DEPTH, {unit: UNITS_LAYER, sets: SETS_LAYER, norm: NORMS_LAYER, pairs: 3 * XPAIRS,
                                  hidden: 2 * GU_ITERS, head: N_HEADS, layers: 1,
                                  branch_pairs: XPAIRS, mixes: 2}):
                ffn()
                mean_square()
                with loop(pe, QKV_ITERS, {unit: 4, sets: 2}):
                    project(xm, xm_lo, pairs)
                    project(xm, xm_lo, pairs)
                with loop(pe, HEAD_ITERS, {unit: 4, sets: 2, head: 1}):
                    head.add()
                    s = new_set()
                    multiply(s, [xm[:, k, :] for k in range(UK)], True, False)
                    wait(pe, (head_copied, head.now))
                    for sm in range(2):
                        half = slice(sm * HEAD_DIM, (sm + 1) * HEAD_DIM)
                        nc.tensor.matmul(score[:, sm, 0:SEQ], head_qkv[half, 0, P:SEQ], head_qkv[half, 1, :],
                                         start=True, stop=True)
                        mm = nc.tensor.matmul(score[:, sm, SEQ:KEYS], head_qkv[half, 0, 0:P],
                                              head_qkv[half, 1, 0:P], start=True, stop=True)
                    mm.then_inc(scored, 1)
                    wait(pe, (pv_read, head.now))
                    for t in range(QT):
                        mm = nc.tensor.transpose(v_ps[:, t * V_DIM:(t + 1) * V_DIM],
                                                 head_qkv[:, 2, t * P:(t + 1) * P], ident[:, :])
                    mm.then_inc(v_turned, 1)
                    multiply(s, [xm[:, k, :] for k in range(UK, KT)], False, True)
                    s = new_set()
                    multiply(s, [xm[:, k, :] for k in range(UK)], True, False)
                    wait(pe, (prob_ready, head.now))
                    for b in range(KEYS // P):
                        mm = nc.tensor.transpose(prob_t_ps[:, b * P:(b + 1) * P], prob[:, b * P:(b + 1) * P],
                                                 ident[:, :])
                    mm.then_inc(prob_turned, 1)
                    multiply(s, [xm[:, k, :] for k in range(UK, KT)], False, True)
                    wait(pe, (v_copied, head.now), (prob_copied, head.now))
                    for k in range(QT):
                        nc.tensor.matmul(pv_ps[:, 1, :], prob_t[:, k * P:(k + 1) * P], v_tok[:, k, :],
                                         start=(k == 0), stop=(k == QT - 1))
                    nc.tensor.matmul(pv_ps[:, 0, :], prob_t[:, SEQ:KEYS], v_tok[:, 0, :], start=True,
                                     stop=True).then_inc(pv_done, 1)
                with loop(pe, UC_ITERS, {unit: 4, sets: 2}):
                    project(xm, xm_lo, pairs)
                    project(xm, xm_lo, pairs)
                layers.add()
                project(xm, xm_lo, pairs)
                wait(pe, (attn_scaled, layers.now))
                for h in range(N_HEADS):
                    for t in range(QT):
                        col = ((h % 2) * QT + t) * P
                        mm = nc.tensor.transpose(side[h // 2][:, col:col + P], attn[:, h, t, :], ident[:, :])
                mm.then_inc(attn_turned, 1)
                project(xm, xm_lo, pairs)
                mixes.add(2)
                with loop(pe, BRANCH_ITERS, {unit: 4, sets: 4}):
                    for j in range(2):
                        for n in range(2):
                            s = new_set()
                            multiply(s, [mix[:, n * UK + k, :] for k in range(UK)], True, True,
                                     (mix_lo, mixes.now - 1 + n))
                branch_pairs.add(XPAIRS)
                with loop(pe, OUT_ITERS, {unit: 4, sets: 2}):
                    project(merged, merged_lo, branch_pairs)
                    project(merged, merged_lo, branch_pairs)
                pairs.add(XPAIRS)
                ffn()
            mean_square()
            pe.wait_ge(y_ready, 1)
            for b in range(4):
                for k in range(2):
                    for t in range(QT):
                        col = (k * QT + t) * P
                        mm = nc.tensor.transpose(side[b][:, col:col + P], xg[:, 2 * b + k, t * P:(t + 1) * P],
                                                 ident[:, :])
                mm.then_inc(y_turned, 1)


_INS = ["x", "norm_ffn1_g", "ffn1_w_gate", "ffn1_w_up", "ffn1_w_down", "norm_mix_g", "w_in", "lambda_q1",
        "lambda_k1", "lambda_q2", "lambda_k2", "subln_g", "rel_bias", "conv_w", "w_branch_attn",
        "w_branch_conv", "w_out", "norm_ffn2_g", "ffn2_w_gate", "ffn2_w_up", "ffn2_w_down", "final_g"]


def kernel(**inputs):
    import numpy as _np
    import concourse.bacc as _bacc
    from concourse import mybir as _mybir
    from concourse.bass_utils import run_bass_kernel_spmd as _run

    nc = _bacc.Bacc("TRN2", target_bir_lowering=False, num_devices=1)
    arrays, args = {}, []
    for name in _INS + ["places"]:
        a = bucket_places() if name == "places" else _np.ascontiguousarray(inputs[name])
        arrays[f"in_{name}_dram"] = a
        args.append(nc.dram_tensor(f"in_{name}_dram", a.shape, _mybir.dt.from_np(a.dtype), kind="ExternalInput").ap())
    out = nc.dram_tensor("out_0_dram", (1, SEQ, D_MODEL), F32, kind="ExternalOutput").ap()
    trunk(nc, *args, out)
    r = _run(nc, [arrays], core_ids=[0])
    return r.results[0]["out_0_dram"]
```

```python
import math
from contextlib import ExitStack, contextmanager

import numpy as np

import concourse.bass as bass
from concourse import mybir

F32 = mybir.dt.float32
F32R = mybir.dt.float32r
ACT = mybir.ActivationFunctionType
ALU = mybir.AluOpType
AX = mybir.AxisListType

P = 128
D_MODEL, SEQ, DEPTH = 1024, 256, 2
HEAD_DIM = 64
V_DIM = 2 * HEAD_DIM
ATTN_W = D_MODEL // 2
N_HEADS = ATTN_W // V_DIM
QK_W = N_HEADS * 2 * HEAD_DIM
CONV_W = D_MODEL // 2
CONV_K = 3
D_FF = (((8 * D_MODEL) // 3 + 255) // 256) * 256
NUM_BUCKETS = 32
MAX_EXACT = NUM_BUCKETS // 2
MAX_DISTANCE = 128
NORM_EPS = 1e-6
SUBLN_EPS = 1e-5
MASKED = -1.0e30

KT = D_MODEL // P
FT = D_FF // P
QT = SEQ // P
PAIR = 2
COLS = PAIR * P
UK = 4
RING = 4
LEAD = 3
ACCS = 2

COL_GATE_ATTN = 2 * QK_W + ATTN_W + 3 * CONV_W
COL_GATE_CONV = COL_GATE_ATTN + D_MODEL
COL_CONV_U = 2 * QK_W + ATTN_W + 2 * CONV_W

GU_ITERS = FT // PAIR
DOWN_UNITS = -(-FT // UK)
DOWN_ITERS = KT // PAIR // 2
QKV_ITERS = (2 * QK_W + ATTN_W) // (2 * COLS)
CONV_T = CONV_W // P
HEAD_ITERS = N_HEADS
UC_ITERS = 2
BRANCH_ITERS = KT // PAIR // 2
OUT_ITERS = KT // PAIR // 2

GU_UNITS, QKV_UNITS = 4, 4
DOWN_BODY = 2 * DOWN_UNITS
UNITS_LAYER = (2 * (GU_ITERS * GU_UNITS + DOWN_ITERS * DOWN_BODY)
               + 4 * (QKV_ITERS + HEAD_ITERS + UC_ITERS + 1 + BRANCH_ITERS + OUT_ITERS))
SETS_LAYER = 2 * 2 * (GU_ITERS + DOWN_ITERS) + 2 * (QKV_ITERS + HEAD_ITERS + UC_ITERS + 1) \
    + 4 * BRANCH_ITERS + 2 * OUT_ITERS
XPAIRS = KT // PAIR
NORMS_LAYER = 3
HEAD_STEPS = 6
STEPS_LAYER = 51

BIAS_ZERO = SEQ - 1
BIAS_LEN = SEQ + P
P_MIX, P_FFN2, P_NEXT, P_CONV, P_SUBLN, P_LAM = 0, KT, 2 * KT, 3 * KT, 3 * KT + CONV_K * CONV_T, \
    3 * KT + CONV_K * CONV_T + 1
PARS = P_LAM + 1


def lambda_init(layer):
    return 0.8 - 0.6 * math.exp(-0.3 * layer)


def bucket_places():
    n = np.arange(SEQ, dtype=np.int32)
    nf = np.maximum(n, MAX_EXACT).astype(np.float32)
    large = MAX_EXACT + (np.log(nf / np.float32(MAX_EXACT)) / np.float32(math.log(MAX_DISTANCE / MAX_EXACT))
                         * np.float32(NUM_BUCKETS - MAX_EXACT)).astype(np.int32)
    bucket = np.where(n < MAX_EXACT, n, np.minimum(large, NUM_BUCKETS - 1))
    places = np.zeros((NUM_BUCKETS, BIAS_LEN), np.float32)
    places[bucket, BIAS_ZERO - n] = 1.0
    return places


def at(t):
    return slice(t, t + PAIR) if isinstance(t, int) else bass.ds(t, PAIR)


class Count:

    def __init__(self, start=0):
        self.fixed, self.moving = start, 0

    def add(self, n=1):
        self.fixed += n
        return self.now

    @property
    def now(self):
        return self.moving + self.fixed


@contextmanager
def loop(eng, n, per, first=0):
    with eng.Fori(first, n) as i:
        before = {c: (c.fixed - first * step, c.moving) for c, step in per.items()}
        for c, step in per.items():
            c.fixed, c.moving = c.fixed - first * step, c.moving + i * step
        yield i
        for c, step in per.items():
            fixed, moving = before[c]
            assert c.fixed - fixed == step, (c.fixed - fixed, step)
            c.fixed, c.moving = fixed + n * step, moving


def wait(eng, *pairs):
    for _, value in pairs:
        if not isinstance(value, int):
            eng.compute_val(value)
    for sem, value in pairs:
        eng.wait_ge(sem, value)


def trunk(nc, x, norm_ffn1_g, ffn1_w_gate, ffn1_w_up, ffn1_w_down, norm_mix_g, w_in,
          lambda_q1, lambda_k1, lambda_q2, lambda_k2, subln_g, rel_bias, conv_w,
          w_branch_attn, w_branch_conv, w_out, norm_ffn2_g, ffn2_w_gate, ffn2_w_up,
          ffn2_w_down, final_g, places, out):
    with ExitStack() as ctx:
        def sb(name, shape, dt=F32):
            return ctx.enter_context(nc.sbuf_tensor(name, [P, *shape], dt))

        def psum(name, shape):
            return ctx.enter_context(nc.psum_tensor(name, [P, *shape], F32))

        def sem(name):
            return ctx.enter_context(nc.semaphore(name))

        raw = sb("raw", [RING, UK, COLS])
        w_hi = sb("w_hi", [RING, UK, COLS], F32R)
        w_lo = sb("w_lo", [RING, UK, COLS], F32R)
        xt = sb("xt", [KT, SEQ])
        xg = sb("xg", [KT, SEQ])
        xm = sb("xm", [KT, 2 * SEQ], F32R)
        hm = sb("hm", [FT, 2 * SEQ], F32R)
        merged = hm[:, 0:KT, :]
        mix = hm[:, KT:2 * KT, :]
        proj = sb("proj", [3 * N_HEADS + 1, SEQ])
        conv_in = proj[:, 0:CONV_T, :]
        conv = proj[:, CONV_T:2 * CONV_T, :]
        gates = sb("gates", [2 * KT, SEQ])
        x_tok = gates[:, 0:KT, :].rearrange("p k n -> p (k n)").rearrange("p (t d) -> p t d", t=QT)
        y_tok = gates[:, KT:2 * KT, :].rearrange("p k n -> p (k n)").rearrange("p (t d) -> p t d", t=QT)
        bias = sb("bias", [N_HEADS, SEQ + P])
        acc_lo = [sb(f"acc_lo{s}", [PAIR, SEQ]) for s in range(ACCS)]
        sums = [sb(f"sum{s}", [PAIR, SEQ]) for s in range(ACCS)]
        silu = sb("silu", [PAIR, SEQ])
        hid = sb("hid", [PAIR, SEQ])
        part = sb("part", [2 * PAIR, SEQ])
        square = sb("square", [PAIR, SEQ])
        square_sum = sb("square_sum", [PAIR, SEQ])
        mean_sq = sb("mean_sq", [SEQ])
        newton = sb("newton", [SEQ])
        inv = sb("inv", [SEQ])
        rstd = sb("rstd", [SEQ])
        half_rstd = sb("half_rstd", [SEQ])
        rstd_square = sb("rstd_square", [SEQ])
        out_ms, out_inv, out_rstd = (sb(n, [QT]) for n in ("out_ms", "out_inv", "out_rstd"))
        KEYS = SEQ + P
        head_qkv = sb("head_qkv", [3, SEQ])
        logits = sb("logits", [2, KEYS])
        expo = sb("expo", [2, KEYS])
        prob = sb("prob", [KEYS])
        row_max = sb("row_max", [QT, 2])
        neg_max = sb("neg_max", [QT, 2])
        row_sum = sb("row_sum", [QT, 2])
        row_inv = sb("row_inv", [QT, 2])
        lam_inv = sb("lam_inv", [QT])
        prob_t = sb("prob_t", [KEYS])
        v_tok = sb("v_tok", [QT, V_DIM])
        attn = sb("attn", [N_HEADS, QT, V_DIM])
        attn_sq = sb("attn_sq", [N_HEADS * QT])
        attn_ms = sb("attn_ms", [N_HEADS * QT])
        attn_inv = sb("attn_inv", [N_HEADS * QT])
        attn_rstd = sb("attn_rstd", [N_HEADS * QT])
        ident = sb("ident", [P])
        mean_ones = sb("mean_ones", [P])
        ones = sb("ones", [P])
        pars = sb("pars", [DEPTH, PARS])
        cur = sb("cur", [PARS])
        first_g = sb("first_g", [KT])
        eps = sb("eps", [1])
        table_probe = sb("table_probe", [4])
        lam_rows = sb("lam_rows", [4, DEPTH * HEAD_DIM])
        lam_prod = sb("lam_prod", [2, DEPTH * HEAD_DIM])
        lam_sum = sb("lam_sum", [2 * DEPTH])
        lam_exp = sb("lam_exp", [2, DEPTH])
        lam_diff = sb("lam_diff", [DEPTH])
        table = sb("table", [N_HEADS])
        onehot = part[:, 0:PAIR, :].rearrange("p k n -> p (k n)")[:, 0:BIAS_LEN]
        table_hi = hm[:, 0, :].rearrange("p (h m) -> p h m", h=N_HEADS)
        table_lo = hm[:, 1, :].rearrange("p (h m) -> p h m", h=N_HEADS)
        onehot_r = hm[:, 2, 0:BIAS_LEN]
        bias_rows = proj[:, 0:2 * N_HEADS, :].rearrange("p k n -> p (k n)")[:, 0:N_HEADS * BIAS_LEN] \
            .rearrange("p (h m) -> p h m", h=N_HEADS)
        bias_dram = nc.dram_tensor("bias_scratch", (N_HEADS, P * BIAS_LEN), F32, kind="Internal").ap()

        acc = [psum(f"acc{s}", [PAIR, 2 * SEQ]) for s in range(ACCS)]
        score = psum("score", [2, 2 * SEQ])
        ps_c = psum("ps_c", [2 * SEQ])
        ps_d = psum("ps_d", [2 * SEQ])
        side = [score[:, 0, :], score[:, 1, :], ps_c[:, :], ps_d[:, :]]
        prob_t_ps = ps_c[:, 0:KEYS]
        v_ps = ps_d[:, 0:QT * V_DIM]
        pv_ps = ps_d[:, SEQ:SEQ + QT * V_DIM].rearrange("p (t d) -> p t d", t=QT)
        msq_ps = ps_c[:, 0:SEQ]
        out_msq_ps = acc[0][:, 0, 0:QT]
        lam_ps = acc[0][:, 0, 0:2 * DEPTH]

        loaded = [sem(f"loaded{s}") for s in range(RING)]
        x_loaded = [sem(f"x_loaded{b}") for b in range(2)]
        gain_loaded, pars_loaded, lam_loaded, table_loaded = (sem(n) for n in (
            "gain_loaded", "pars_loaded", "lam_loaded", "table_loaded"))
        bias_stored, bias_loaded, out_stored = sem("bias_stored"), sem("bias_loaded"), sem("out_stored")
        hi_split = sem("hi_split")
        lo_split = sem("lo_split")
        used = sem("used")
        acc_copied = sem("acc_copied")
        acc_summed = sem("acc_summed")
        gate_ready, silu_done, hid_ready, hid_hi, hid_lo = (sem(n) for n in (
            "gate_ready", "silu_done", "hid_ready", "hid_hi", "hid_lo"))
        x_new, squared, square_added, xg_ready, xm_hi, xm_lo = (sem(n) for n in (
            "x_new", "squared", "square_added", "xg_ready", "xm_hi", "xm_lo"))
        msq_summed, msq_ready, inv_ready = (sem(n) for n in ("msq_summed", "msq_ready", "inv_ready"))
        scored, max_ready, exp_done, prob_ready, prob_turned, prob_copied = (sem(n) for n in (
            "scored", "max_ready", "exp_done", "prob_ready", "prob_turned", "prob_copied"))
        proj_ready, head_copied = sem("proj_ready"), sem("head_copied")
        v_turned, v_copied, pv_done, pv_read = (sem(n) for n in ("v_turned", "v_copied", "pv_done", "pv_read"))
        attn_squared, attn_rstd_ready = sem("attn_squared"), sem("attn_rstd_ready")
        conv_in_ready, conv_started = sem("conv_in_ready"), sem("conv_started")
        out_rstd_ready, pars_ready, onehot_ready = (sem(n) for n in ("out_rstd_ready", "pars_ready", "onehot_ready"))
        attn_ms_ready, attn_inv_ready, attn_scaled, attn_turned, attn_gained, attn_hi = (sem(n) for n in (
            "attn_ms_ready", "attn_inv_ready", "attn_scaled", "attn_turned", "attn_gained", "attn_hi"))
        mix_lo, conv_ready, conv_hi = sem("mix_lo"), sem("conv_ready"), sem("conv_hi")
        gates_done, merged_ready, merged_hi, merged_lo = (sem(n) for n in (
            "gates_done", "merged_ready", "merged_hi", "merged_lo"))
        vec_step, act_step = sem("vec_step"), sem("act_step")
        ident_zeroed, ident_ready, ones_ready = sem("ident_zeroed"), sem("ident_ready"), sem("ones_ready")
        x_turned, lam_summed, lam_spread, lam_exped = (sem(n) for n in (
            "x_turned", "lam_summed", "lam_spread", "lam_exped"))
        table_ready, bias_spread, bias_rows_ready = sem("table_ready"), sem("bias_spread"), sem("bias_rows_ready")
        bias_copied, lam_diffed = sem("bias_copied"), sem("lam_diffed")
        y_ready, y_turned, y_copied = sem("y_ready"), sem("y_turned"), sem("y_copied")

        def wide(v):
            return v.unsqueeze(1).to_broadcast([P, PAIR, SEQ])

        block = ctx.enter_context(nc.Block())

        @block.sync
        def _(sp):
            split = Count(1)
            slot = [0]

            def load(src):
                s = slot[0] % RING
                sp.lower_ap_dma(src)
                wait(sp, (lo_split, split.now))
                sp.dma_start(raw[:, s, 0:src.shape[1], :], src).then_inc(loaded[s], 16)
                split.add()
                slot[0] += 1

            def rows(w, l):
                return w[bass.ds(l, 1)].rearrange("o (k p) n -> p (o k) n", p=P)

            def both(l, wa, a, wb, b):
                for k in range(0, KT, UK):
                    load(rows(wa, l)[:, k:k + UK, bass.ds(a, COLS)])
                    load(rows(wb, l)[:, k:k + UK, bass.ds(b, COLS)])

            def down(w, l, col):
                for k in range(0, FT, UK):
                    load(rows(w, l)[:, k:min(k + UK, FT), bass.ds(col, COLS)])

            for b in range(2):
                half = slice(b * D_MODEL // 2, (b + 1) * D_MODEL // 2)
                sp.dma_start(x_tok[:, :, half],
                             x[0].rearrange("(t p) d -> p t d", p=P)[:, :, half]).then_inc(x_loaded[b], 16)

            with loop(sp, DEPTH, {split: UNITS_LAYER}) as l:
                with loop(sp, GU_ITERS, {split: GU_UNITS}) as i:
                    both(l, ffn1_w_gate, i * COLS, ffn1_w_up, i * COLS)
                with loop(sp, DOWN_ITERS, {split: DOWN_BODY}) as i:
                    for j in range(2):
                        down(ffn1_w_down, l, i * (2 * COLS) + j * COLS)
                with loop(sp, QKV_ITERS, {split: 4}) as i:
                    both(l, w_in, i * (2 * COLS), w_in, i * (2 * COLS) + COLS)
                with loop(sp, HEAD_ITERS, {split: 4}) as i:
                    both(l, w_in, i * COLS + COL_GATE_ATTN, w_in, i * COLS + COL_GATE_CONV)
                with loop(sp, UC_ITERS + 1, {split: 4}) as i:
                    both(l, w_in, COL_CONV_U - i * CONV_W, w_in, COL_CONV_U + COLS - i * CONV_W)
                with loop(sp, BRANCH_ITERS, {split: 4}) as i:
                    for w in (w_branch_attn, w_branch_conv):
                        for j in range(2):
                            load(rows(w, l)[:, :, bass.ds(i * (2 * COLS) + j * COLS, COLS)])
                with loop(sp, OUT_ITERS, {split: 4}) as i:
                    both(l, w_out, i * (2 * COLS), w_out, i * (2 * COLS) + COLS)
                with loop(sp, GU_ITERS, {split: GU_UNITS}) as i:
                    both(l, ffn2_w_gate, i * COLS, ffn2_w_up, i * COLS)
                with loop(sp, DOWN_ITERS, {split: DOWN_BODY}) as i:
                    for j in range(2):
                        down(ffn2_w_down, l, i * (2 * COLS) + j * COLS)
            for n in range(LEAD):
                wait(sp, (lo_split, split.now + n))
                sp.sem_inc(loaded[n], 16)

            for b in range(XPAIRS):
                sp.wait_ge(y_copied, b + 1)
                sp.dma_start(out[0].rearrange("(t p) d -> p t d", p=P)[:, :, b * COLS:(b + 1) * COLS],
                             y_tok[:, :, b * COLS:(b + 1) * COLS]).then_inc(out_stored, 16)
            sp.wait_ge(out_stored, 16 * XPAIRS)

        @block.gpsimd
        def _(pool):
            nc.gpsimd.memset(ident[:, :], 0.0).then_inc(ident_zeroed, 1)
            nc.gpsimd.memset(mean_ones[:, :], 1.0 / D_MODEL).then_inc(ones_ready, 1)
            nc.gpsimd.memset(ones[:, :], 1.0).then_inc(ones_ready, 1)
            pool.wait_ge(ident_zeroed, 1)
            nc.gpsimd.affine_select(out=ident[:, :], in_=ident[:, :], compare_op=ALU.not_equal, fill=1.0,
                                    base=0, pattern=[[-1, P]], channel_multiplier=1).then_inc(ident_ready, 1)
            nc.gpsimd.memset(proj[:, 3 * N_HEADS, :], 0.0).then_inc(ones_ready, 1)
            nc.gpsimd.memset(eps[:, :], SUBLN_EPS).then_inc(ones_ready, 1)
            pool.wait_ge(bias_copied, 1)
            nc.gpsimd.memset(bias_rows[:, :, BIAS_ZERO + 1:], MASKED).then_inc(bias_rows_ready, 1)
            pool.wait_ge(bias_rows_ready, 1)
            pool.dma_start(bias_dram.rearrange("h (p m) -> p h m", p=P), bias_rows).then_inc(bias_stored, 16)
            pool.wait_ge(bias_stored, 16)
            back = bias_dram[:, P - 1:P - 1 + P * (BIAS_LEN - 1)].rearrange("h (p m) -> p h m", p=P)
            pool.dma_start(bias[:, :, 0:SEQ], back[:, :, 0:SEQ]).then_inc(bias_loaded, 16)
            pool.dma_start(bias[:, :, SEQ:], back[:, :, P:SEQ]).then_inc(bias_loaded, 16)
            pool.wait_ge(lam_exped, 1)
            nc.gpsimd.tensor_tensor(lam_diff[:, :], lam_exp[:, 0, :], lam_exp[:, 1, :],
                                    ALU.subtract).then_inc(lam_diffed, 1)
            pool.wait_ge(lam_diffed, 1)
            pool.wait_ge(pars_loaded, 16 * DEPTH * (4 + CONV_K))
            for l in range(DEPTH):
                nc.gpsimd.tensor_scalar(pars[:, l, P_LAM:P_LAM + 1], lam_diff[:, l:l + 1], lambda_init(l),
                                        None, ALU.add)
                nc.gpsimd.tensor_scalar(pars[:, l, P_SUBLN:P_SUBLN + 1], pars[:, l, P_SUBLN:P_SUBLN + 1],
                                        1.0 - lambda_init(l), None, ALU.mult).then_inc(pars_ready, 1)
            pool.wait_ge(bias_loaded, 32)

        @block.scalar
        def _(act):
            split = Count()
            loads = Count()
            sets = Count()
            pair = Count()
            norm = Count()
            hidden = Count()
            head = Count()
            projs = Count()
            layers = Count()
            conv_pairs = Count()
            branch_pairs = Count()
            probes = Count()
            spare = act.alloc_register("spare")
            slot = [0]
            units_done = Count(RING)

            def hi(tiles=UK):
                s = slot[0] % RING
                wait(act, (loaded[s], loads.now + 16), (used, split.now + 1))
                nc.scalar.copy(w_hi[:, s, 0:tiles, :], raw[:, s, 0:tiles, :]).then_inc(hi_split, 1)
                split.add()
                slot[0] += 1
                if slot[0] % RING == 0:
                    loads.add(16)

            def copy_acc(units):
                s = sets.fixed % ACCS
                units_done.add(units)
                wait(act, (used, units_done.now), (acc_summed, sets.now + 1))
                nc.scalar.copy(acc_lo[s][:, :, :], acc[s][:, :, SEQ:2 * SEQ]).then_inc(acc_copied, 1)
                sets.add()

            def moving_x(t, moving):
                pair.add()
                wait(act, (x_new, pair.now))
                if moving:
                    act.reg_mov(spare, 0)
                nc.scalar.activation(square[:, :, :], xt[:, at(t), :], ACT.Square).then_inc(squared, 1)
                wait(act, (xg_ready, pair.now))
                if moving:
                    act.reg_mov(spare, 0)
                nc.scalar.copy(xm[:, at(t), 0:SEQ], xg[:, at(t), :]).then_inc(xm_hi, 1)

            def norm_root():
                norm.add()
                wait(act, (msq_ready, norm.now))
                nc.scalar.activation(inv[:, :], mean_sq[:, :], ACT.Abs_reciprocal_sqrt).then_inc(inv_ready, 1)

            def have_table(function):
                nc.scalar.activation(table_probe[:, probes.now:probes.now + 1], eps[:, :], function)
                probes.add()

            def two_sets(between=None):
                hi()
                hi()
                hi()
                if between:
                    between()
                copy_acc(3)
                hi()
                copy_acc(1)

            def ffn():
                def gate_up(i, first):
                    hi()
                    hi()
                    hi()
                    if first:
                        norm_root()
                    copy_acc(3)
                    hi()
                    hidden.add()
                    wait(act, (gate_ready, hidden.now))
                    nc.scalar.activation(silu[:, :, :], sums[0][:, :, :], ACT.Silu).then_inc(silu_done, 1)
                    copy_acc(1)
                    wait(act, (hid_ready, hidden.now))
                    if not first:
                        act.reg_mov(spare, 0)
                    nc.scalar.copy(hm[:, at(i * PAIR), 0:SEQ], hid[:, :, :]).then_inc(hid_hi, 1)

                gate_up(0, True)
                with loop(act, GU_ITERS, {split: 4, loads: 16, sets: 2, units_done: 4, hidden: 1}, 1) as i:
                    gate_up(i, False)
                with loop(act, DOWN_ITERS, {split: 12, loads: 48, sets: 2, units_done: 12, pair: 2}) as i:
                    for j in range(2):
                        for k in range(DOWN_UNITS):
                            u = k + LEAD
                            hi(FT - UK * (DOWN_UNITS - 1) if u == DOWN_UNITS - 1 else UK)
                        copy_acc(DOWN_UNITS)
                        moving_x(i * (2 * PAIR) + j * PAIR, True)

            def columns(v):
                return v.rearrange("(k p) -> p k", p=P)

            def par(l, at, src):
                act.dma_start(pars[:, l, at:at + src.shape[1]], src,
                              allow_slow_non_contiguous=True).then_inc(pars_loaded, 16)

            act.dma_start(table[0:NUM_BUCKETS, :], rel_bias).then_inc(table_loaded, 16)
            act.dma_start(onehot[0:NUM_BUCKETS, :], places).then_inc(table_loaded, 16)
            act.dma_start(first_g[:, :], columns(norm_ffn1_g[0]), allow_slow_non_contiguous=True) \
                .then_inc(gain_loaded, 16)
            for n, v in enumerate((lambda_q1, lambda_k1, lambda_q2, lambda_k2)):
                act.dma_start(lam_rows[0:1, n, :], v.rearrange("(o l) d -> o (l d)", o=1)).then_inc(lam_loaded, 16)
            act.wait_ge(table_loaded, 32)
            nc.scalar.copy(onehot_r[0:NUM_BUCKETS, :], onehot[0:NUM_BUCKETS, :]).then_inc(onehot_ready, 1)
            act.wait_ge(ones_ready, 4)
            have_table(ACT.Exp)
            wait(act, (lam_spread, 1))
            nc.scalar.activation(lam_exp[:, :, :], lam_ps.rearrange(
                "p (s l) -> p s l", s=2), ACT.Exp).then_inc(lam_exped, 1)
            have_table(ACT.Silu)
            for p in range(XPAIRS):
                if p:
                    act.wait_ge(square_added, p)
                moving_x(p * PAIR, False)
                if p < LEAD:
                    hi()
            act.wait_ge(bias_spread, 1)
            for h in range(N_HEADS):
                last = nc.scalar.copy(bias_rows[:, h, :], side[h][:, 0:BIAS_LEN])
            last.then_inc(bias_copied, 1)
            for l in range(DEPTH):
                par(l, P_MIX, columns(norm_mix_g[l]))
                par(l, P_FFN2, columns(norm_ffn2_g[l]))
                par(l, P_NEXT, columns(norm_ffn1_g[l + 1] if l + 1 < DEPTH else final_g))
                par(l, P_SUBLN, columns(subln_g[l]))
                for k in range(CONV_K):
                    par(l, P_CONV + k * CONV_T, columns(conv_w[l, k]))
            with loop(act, DEPTH, {split: UNITS_LAYER, loads: 4 * UNITS_LAYER, sets: SETS_LAYER,
                                   units_done: UNITS_LAYER, pair: 3 * XPAIRS, norm: NORMS_LAYER,
                                   hidden: 2 * GU_ITERS, head: N_HEADS, projs: 2 * QKV_ITERS, layers: 1,
                                   conv_pairs: 2, branch_pairs: XPAIRS}):
                ffn()
                two_sets(norm_root)
                with loop(act, QKV_ITERS, {split: 4, loads: 16, sets: 2, units_done: 4}, 1):
                    two_sets()
                projs.add(2 * QKV_ITERS)
                have_table(ACT.Exp)

                wait(act, (proj_ready, projs.now))
                nc.scalar.copy(head_qkv[:, :, :], proj[:, 0:3 * N_HEADS, :].rearrange(
                    "p (a h) n -> p h a n", a=3)[:, 0]).then_inc(head_copied, 1)
                with loop(act, HEAD_ITERS, {split: 4, loads: 16, sets: 2, units_done: 4, head: 1}) as h:
                    head.add()
                    hi()
                    hi()
                    wait(act, (v_turned, head.now))
                    nc.scalar.copy(v_tok[:, :, :].rearrange("p t d -> p (t d)"), v_ps).then_inc(v_copied, 1)
                    wait(act, (max_ready, head.now))
                    for t, (a, b) in enumerate(((SEQ, KEYS), (0, SEQ))):
                        for s in range(2):
                            last = nc.scalar.activation(expo[:, s, a:b], logits[:, s, a:b], ACT.Exp,
                                                        bias=neg_max[:, t, s:s + 1],
                                                        accum_out=row_sum[:, t, s:s + 1])
                    last.then_inc(exp_done, 1)
                    hi()
                    copy_acc(3)
                    hi()
                    copy_acc(1)
                    wait(act, (prob_turned, head.now))
                    nc.scalar.copy(prob_t[:, :], prob_t_ps).then_inc(prob_copied, 1)
                    nc.scalar.copy(head_qkv[:, :, :], proj[:, 1:3 * N_HEADS + 1, :].rearrange(
                        "p (a h) n -> p h a n", a=3)[:, bass.ds(h, 1)].rearrange(
                            "p o a n -> p (o a) n")).then_inc(head_copied, 1)
                    wait(act, (pv_done, head.now))
                    act.reg_mov(spare, 0)
                    nc.scalar.copy(attn[:, bass.ds(h, 1)].rearrange("p o t d -> p (o t) d"),
                                   pv_ps).then_inc(pv_read, 1)
                layers.add()
                hi()
                hi()
                wait(act, (pv_read, head.now + 1))
                for h in range(N_HEADS):
                    for t in range(QT):
                        n = h * QT + t
                        last = nc.scalar.activation(xg[:, n // 2, (n % 2) * V_DIM:(n % 2 + 1) * V_DIM],
                                                    attn[:, h, t, :], ACT.Square, accum_out=attn_sq[:, n:n + 1])
                last.then_inc(attn_squared, 1)
                hi()
                copy_acc(3)
                hi()
                copy_acc(1)
                hi()
                wait(act, (attn_ms_ready, layers.now))
                nc.scalar.activation(attn_inv[:, :], attn_ms[:, :],
                                     ACT.Abs_reciprocal_sqrt).then_inc(attn_inv_ready, 1)
                hi()
                hi()
                wait(act, (attn_rstd_ready, layers.now))
                for h in range(N_HEADS):
                    for t in range(QT):
                        n = h * QT + t
                        last = nc.scalar.activation(attn[:, h, t, :], attn[:, h, t, :], ACT.Copy,
                                                    scale=attn_rstd[:, n:n + 1])
                last.then_inc(attn_scaled, 1)
                copy_acc(3)
                hi()
                copy_acc(1)
                hi()
                wait(act, (conv_in_ready, 2 * layers.now))
                for t in range(CONV_T):
                    tap = P_CONV + (CONV_K - 1) * CONV_T + t
                    last = nc.scalar.activation(conv[:, t, :], conv_in[:, t, :], ACT.Copy, scale=cur[:, tap:tap + 1])
                last.then_inc(conv_started, 1)
                hi()
                wait(act, (attn_turned, layers.now))
                for b in range(2):
                    last = nc.scalar.activation(
                        attn[:, 2 * b:2 * b + 2].rearrange("p h t d -> p (h t d)"), side[b], ACT.Copy,
                        scale=cur[:, P_SUBLN:P_SUBLN + 1])
                last.then_inc(attn_gained, 1)
                hi()
                wait(act, (attn_gained, layers.now))
                nc.scalar.copy(mix[:, 0:N_HEADS, 0:SEQ],
                               attn[:, :, :, :].rearrange("p h t d -> p h (t d)")).then_inc(attn_hi, 1)
                copy_acc(3)
                hi()
                have_table(ACT.Sigmoid)
                for j in range(2):
                    if j:
                        copy_acc(1)
                    conv_pairs.add()
                    wait(act, (conv_ready, conv_pairs.now))
                    nc.scalar.copy(mix[:, N_HEADS + j * PAIR:N_HEADS + (j + 1) * PAIR, 0:SEQ],
                                   conv[:, j * PAIR:(j + 1) * PAIR, :]).then_inc(conv_hi, 1)
                with loop(act, BRANCH_ITERS, {split: 4, loads: 16, sets: 4, units_done: 4, branch_pairs: 2}) as i:
                    for g in range(2):
                        g_at = gates[:, bass.ds(i * (2 * PAIR) + g * KT, 2 * PAIR), :]
                        nc.scalar.activation(g_at, g_at, ACT.Sigmoid).then_inc(gates_done, 1)
                    hi()
                    copy_acc(1)
                    hi()
                    copy_acc(1)
                    hi()
                    copy_acc(1)
                    hi()
                    for j in range(2):
                        if j:
                            copy_acc(1)
                        branch_pairs.add()
                        wait(act, (merged_ready, branch_pairs.now))
                        act.reg_mov(spare, 0)
                        nc.scalar.copy(merged[:, bass.ds(i * (2 * PAIR) + j * PAIR, PAIR), 0:SEQ],
                                       part[:, j * PAIR:(j + 1) * PAIR, :]).then_inc(merged_hi, 1)
                with loop(act, OUT_ITERS, {split: 4, loads: 16, sets: 2, units_done: 4, pair: 2}) as i:
                    hi()
                    hi()
                    hi()
                    copy_acc(3)
                    moving_x(i * (2 * PAIR), True)
                    hi()
                    copy_acc(1)
                    moving_x(i * (2 * PAIR) + PAIR, True)
                ffn()
            wait(act, (msq_ready, norm.now + 1))
            nc.scalar.activation(out_inv[:, :], out_ms[:, :], ACT.Abs_reciprocal_sqrt).then_inc(inv_ready, 1)
            wait(act, (out_rstd_ready, 1))
            for b in range(XPAIRS):
                act.wait_ge(y_turned, b + 1)
                for t in range(QT):
                    last = nc.scalar.activation(
                        y_tok[:, t, b * COLS:(b + 1) * COLS].rearrange("p (k d) -> p k d", k=PAIR),
                        side[b].rearrange("p (k t d) -> p k t d", k=PAIR, t=QT)[:, :, t], ACT.Copy,
                        scale=out_rstd[:, t:t + 1])
                last.then_inc(y_copied, 1)

        @block.vector
        def _(dve):
            split = Count()
            sets = Count()
            pair = Count()
            norm = Count()
            hidden = Count()
            head = Count()
            layers = Count()
            branch_pairs = Count()
            conv_pairs = Count()
            gated = Count()
            step = Count()
            slot = [0]

            def own(ins):
                ins.then_inc(vec_step, 1)
                step.add()
                wait(dve, (vec_step, step.now))

            def lo(tiles=UK):
                s = slot[0] % RING
                wait(dve, (hi_split, split.now + 1))
                nc.vector.tensor_tensor(w_lo[:, s, 0:tiles, :], raw[:, s, 0:tiles, :], w_hi[:, s, 0:tiles, :],
                                        ALU.subtract).then_inc(lo_split, 1)
                split.add()
                slot[0] += 1

            def sum_acc(out=None):
                s = sets.fixed % ACCS
                sets.add()
                out = sums[s][:, :, :] if out is None else out
                wait(dve, (acc_copied, sets.now))
                nc.vector.tensor_tensor(out, acc[s][:, :, 0:SEQ], acc_lo[s][:, :, :],
                                        ALU.add).then_inc(acc_summed, 1)
                wait(dve, (acc_summed, sets.now + ACCS))
                return out

            def moving_x(t, gains):
                pair.add()
                x_at, g_at, m_at = (v[:, at(t), :] for v in (xt, xg, xm))
                gain = gains.unsqueeze(2).to_broadcast([P, PAIR, SEQ])
                for ap in (x_at, g_at, gain, m_at[:, :, 0:SEQ], m_at[:, :, SEQ:2 * SEQ]):
                    dve.lower_ap(ap)
                wait(dve, (x_new, pair.now))
                nc.vector.tensor_tensor(g_at, x_at, gain, ALU.mult).then_inc(xg_ready, 1)
                wait(dve, (squared, pair.now))
                nc.vector.tensor_tensor(square_sum[:, :, :], square_sum[:, :, :], square[:, :, :],
                                        ALU.add).then_inc(square_added, 1)
                wait(dve, (xm_hi, pair.now))
                nc.vector.tensor_tensor(m_at[:, :, SEQ:2 * SEQ], g_at, m_at[:, :, 0:SEQ],
                                        ALU.subtract).then_inc(xm_lo, 1)

            def norm_start():
                norm.add()
                wait(dve, (msq_summed, norm.now))
                nc.vector.memset(square_sum[:, :, :], 0.0)
                nc.vector.tensor_scalar(mean_sq[:, :], msq_ps, NORM_EPS, None, ALU.add).then_inc(msq_ready, 1)

            def refine(result, start, square):
                t = newton[:, 0:square.shape[1]]
                own(nc.vector.scalar_tensor_tensor(out=t, in0=start, scalar=-0.5, in1=start, op0=ALU.mult,
                                                   op1=ALU.mult))
                own(nc.vector.tensor_tensor(t, t, square, ALU.mult))
                own(nc.vector.scalar_tensor_tensor(out=result, in0=t, scalar=1.5, in1=start, op0=ALU.add,
                                                   op1=ALU.mult))

            def norm_rstd():
                wait(dve, (inv_ready, norm.now))
                refine(rstd[:, :], inv[:, :], mean_sq[:, :])

            def scaled(target, by):
                summed = sum_acc()
                return nc.vector.tensor_tensor(target, summed, wide(by[:, :]), ALU.mult)

            def ffn(g_next, new_layer=None):
                def gate_up(i, first):
                    lo()
                    lo()
                    if first:
                        norm_start()
                    lo()
                    if first:
                        norm_rstd()
                        nc.vector.tensor_scalar(half_rstd[:, :], rstd[:, :], 0.5, None, ALU.mult)
                    scaled(sums[0][:, :, :], rstd).then_inc(gate_ready, 1)
                    lo()
                    hidden.add()
                    h_at = hm[:, at(i * PAIR), :]
                    if not first:
                        for ap in (h_at[:, :, 0:SEQ], h_at[:, :, SEQ:2 * SEQ]):
                            dve.lower_ap(ap)
                    up = sum_acc()
                    wait(dve, (silu_done, hidden.now))
                    nc.vector.tensor_tensor(hid[:, :, :], up, silu[:, :, :],
                                            ALU.mult).then_inc(hid_ready, 1)
                    wait(dve, (hid_hi, hidden.now))
                    nc.vector.tensor_tensor(h_at[:, :, SEQ:2 * SEQ], hid[:, :, :], h_at[:, :, 0:SEQ],
                                            ALU.subtract).then_inc(hid_lo, 1)

                gate_up(0, True)
                with loop(dve, GU_ITERS, {split: 4, sets: 2, hidden: 1, step: 0}, 1) as i:
                    gate_up(i, False)
                if new_layer is not None:
                    par_at = pars[:, bass.ds(new_layer, 1), :].rearrange("p o n -> p (o n)")
                    dve.wait_ge(pars_ready, DEPTH)
                    nc.vector.tensor_copy(cur[:, :], par_at)
                with loop(dve, DOWN_ITERS, {split: 12, sets: 2, pair: 2, step: 2}) as i:
                    for j in range(2):
                        for k in range(DOWN_UNITS):
                            u = k + LEAD
                            lo(FT - UK * (DOWN_UNITS - 1) if u == DOWN_UNITS - 1 else UK)
                        t = i * (2 * PAIR) + j * PAIR
                        x_at = xt[:, at(t), :]
                        dve.lower_ap(x_at)
                        summed = sum_acc()
                        own(nc.vector.tensor_tensor(summed, summed, wide(half_rstd[:, :]),
                                                    ALU.mult))
                        nc.vector.tensor_tensor(x_at, x_at, summed, ALU.add).then_inc(x_new, 1)
                        moving_x(t, cur[:, bass.ds(i * (2 * PAIR) + (g_next + j * PAIR), PAIR)])

            dve.sem_inc(used, RING)
            dve.sem_inc(lo_split, RING)
            dve.sem_inc(acc_summed, ACCS)
            dve.sem_inc(pv_read, 1)
            nc.vector.memset(square_sum[:, :, :], 0.0)
            dve.wait_ge(lam_loaded, 64)
            for s in range(2):
                last = nc.vector.tensor_tensor(lam_prod[0:1, s, :], lam_rows[0:1, 2 * s, :],
                                               lam_rows[0:1, 2 * s + 1, :], ALU.mult)
            own(last)
            nc.vector.tensor_reduce(
                lam_sum[0:1, :], lam_prod[0:1, :, :].rearrange("p s (l d) -> p (s l) d", l=DEPTH),
                AX.X, ALU.add).then_inc(lam_summed, 1)
            dve.wait_ge(table_loaded, 32)
            table_at = table[0:NUM_BUCKETS, :].unsqueeze(2).to_broadcast([NUM_BUCKETS, N_HEADS, P])
            own(nc.vector.tensor_copy(table_hi[0:NUM_BUCKETS, :, :], table_at))
            nc.vector.tensor_tensor(table_lo[0:NUM_BUCKETS, :, :], table_at, table_hi[0:NUM_BUCKETS, :, :],
                                    ALU.subtract).then_inc(table_ready, 1)
            dve.wait_ge(gain_loaded, 16)
            for p in range(XPAIRS):
                if p % 2 == 0:
                    for q in (p, p + 1):
                        dve.wait_ge(x_turned, q + 1)
                        nc.vector.tensor_copy(xt[:, 2 * q:2 * q + 2, :].rearrange("p k n -> p (k n)"),
                                              acc[q // 2][:, q % 2, :]).then_inc(x_new, 1)
                moving_x(p * PAIR, first_g[:, p * PAIR:(p + 1) * PAIR])
                if p < LEAD:
                    lo()
            with loop(dve, DEPTH, {split: UNITS_LAYER, sets: SETS_LAYER, pair: 3 * XPAIRS, norm: NORMS_LAYER,
                                   hidden: 2 * GU_ITERS, head: N_HEADS, layers: 1, branch_pairs: XPAIRS,
                                   conv_pairs: 2, gated: 2 * BRANCH_ITERS, step: STEPS_LAYER}) as l:
                ffn(P_MIX, l)
                def two_pairs(i, first):
                    lo()
                    lo()
                    if first:
                        norm_start()
                    lo()
                    if first:
                        norm_rstd()
                    for j in range(2):
                        p_at = proj[:, at(i * (2 * PAIR) + j * PAIR), :]
                        if not first:
                            dve.lower_ap(p_at)
                        scaled(p_at, rstd).then_inc(proj_ready, 1)
                        if j == 0:
                            lo()

                two_pairs(0, True)
                with loop(dve, QKV_ITERS, {split: 4, sets: 2}, 1) as i:
                    two_pairs(i, False)
                nc.vector.tensor_tensor(rstd_square[:, :], rstd[:, :], rstd[:, :], ALU.mult)
                dve.wait_ge(bias_loaded, 32)
                with loop(dve, HEAD_ITERS, {split: 4, sets: 2, head: 1, step: HEAD_STEPS}) as h:
                    head.add()
                    lo()
                    b_at = bias[:, bass.ds(h, 1), :].to_broadcast([P, 2, KEYS])
                    dve.lower_ap(b_at)
                    wait(dve, (scored, head.now))
                    own(nc.vector.scalar_tensor_tensor(out=logits[:, :, :], in0=score[:, :, 0:KEYS],
                                                       scalar=HEAD_DIM ** -0.5, in1=b_at, op0=ALU.mult,
                                                       op1=ALU.add))
                    nc.vector.tensor_reduce(row_max[:, 1, :], logits[:, :, 0:SEQ], AX.X, ALU.max)
                    own(nc.vector.tensor_reduce(row_max[:, 0, :], logits[:, :, SEQ:], AX.X, ALU.max))
                    nc.vector.tensor_scalar(neg_max[:, :, :], row_max[:, :, :], -1.0, None,
                                            ALU.mult).then_inc(max_ready, 1)
                    lo()
                    lo()
                    wait(dve, (exp_done, head.now))
                    own(nc.vector.reciprocal(row_inv[:, :, :], row_sum[:, :, :]))
                    own(nc.vector.tensor_scalar(lam_inv[:, :], row_inv[:, :, 1], cur[:, P_LAM:P_LAM + 1], None,
                                                ALU.mult))
                    for t, (a, b) in enumerate(((SEQ, KEYS), (0, SEQ))):
                        own(nc.vector.tensor_scalar(expo[:, 1, a:b], expo[:, 1, a:b], lam_inv[:, t:t + 1], None,
                                                    ALU.mult))
                        last = nc.vector.scalar_tensor_tensor(
                            out=prob[:, a:b], in0=expo[:, 0, a:b], scalar=row_inv[:, t, 0:1], in1=expo[:, 1, a:b],
                            op0=ALU.mult, op1=ALU.subtract)
                    last.then_inc(prob_ready, 1)
                    g_at = gates[:, bass.ds(h * PAIR, PAIR), :]
                    dve.lower_ap(g_at)
                    scaled(g_at, rstd)
                    lo()
                    g_at = gates[:, bass.ds(h * PAIR + KT, PAIR), :]
                    dve.lower_ap(g_at)
                    scaled(g_at, rstd)
                layers.add()
                lo()
                lo()
                lo()
                wait(dve, (attn_squared, layers.now))
                nc.vector.tensor_scalar(attn_ms[:, :], attn_sq[:, :], 1.0 / V_DIM, SUBLN_EPS,
                                        ALU.mult, ALU.add).then_inc(attn_ms_ready, 1)
                scaled(conv_in[:, 0:PAIR, :], rstd_square)
                lo()
                scaled(conv_in[:, PAIR:2 * PAIR, :], rstd_square)
                lo()
                wait(dve, (attn_inv_ready, layers.now))
                refine(attn_rstd[:, :], attn_inv[:, :], attn_ms[:, :])
                dve.sem_inc(attn_rstd_ready, 1)
                lo()
                lo()
                for j in range(2):
                    u_at = conv_in[:, j * PAIR:(j + 1) * PAIR, :]
                    summed = sum_acc()
                    nc.vector.tensor_tensor(u_at, u_at, summed, ALU.mult).then_inc(conv_in_ready, 1)
                    if j == 0:
                        lo()
                wait(dve, (conv_in_ready, 2 * layers.now))
                lo()
                lo()
                wait(dve, (conv_started, layers.now))
                for k in range(CONV_K - 1):
                    d = CONV_K - 1 - k
                    for t in range(CONV_T):
                        tap = P_CONV + k * CONV_T + t
                        last = nc.vector.scalar_tensor_tensor(
                            out=conv[:, t, d:], in0=conv_in[:, t, 0:SEQ - d], scalar=cur[:, tap:tap + 1],
                            in1=conv[:, t, d:], op0=ALU.mult, op1=ALU.add)
                    own(last)
                own(nc.vector.tensor_tensor(conv, conv, rstd[:, :].unsqueeze(1).to_broadcast([P, CONV_T, SEQ]),
                                            ALU.mult))
                lo()
                wait(dve, (attn_hi, layers.now))
                nc.vector.tensor_tensor(mix[:, 0:N_HEADS, SEQ:2 * SEQ],
                                        attn[:, :, :, :].rearrange("p h t d -> p h (t d)"),
                                        mix[:, 0:N_HEADS, 0:SEQ], ALU.subtract).then_inc(mix_lo, 1)
                for j in range(2):
                    pair_at = slice(j * PAIR, (j + 1) * PAIR)
                    summed = sum_acc()
                    nc.vector.tensor_tensor(conv[:, pair_at, :], conv[:, pair_at, :], summed,
                                            ALU.mult).then_inc(conv_ready, 1)
                    if j == 0:
                        lo()
                    conv_pairs.add()
                    wait(dve, (conv_hi, conv_pairs.now))
                    nc.vector.tensor_tensor(mix[:, N_HEADS + j * PAIR:N_HEADS + (j + 1) * PAIR, SEQ:2 * SEQ],
                                            conv[:, pair_at, :],
                                            mix[:, N_HEADS + j * PAIR:N_HEADS + (j + 1) * PAIR, 0:SEQ],
                                            ALU.subtract).then_inc(mix_lo, 1)
                with loop(dve, BRANCH_ITERS, {split: 4, sets: 4, branch_pairs: 2, gated: 2, step: 2}) as i:
                    for g in range(2):
                        gated.add()
                        for j in range(2):
                            lo()
                            g_at = gates[:, bass.ds(i * (2 * PAIR) + (g * KT + j * PAIR), PAIR), :]
                            p_at = part[:, j * PAIR:(j + 1) * PAIR, :]
                            dve.lower_ap(g_at)
                            summed = sum_acc()
                            if j == 0:
                                wait(dve, (gates_done, gated.now))
                            if g == 0:
                                nc.vector.tensor_tensor(p_at, summed, g_at, ALU.mult)
                            else:
                                own(nc.vector.tensor_tensor(summed, summed, g_at, ALU.mult))
                                nc.vector.tensor_tensor(p_at, p_at, summed, ALU.add).then_inc(merged_ready, 1)
                    for j in range(2):
                        branch_pairs.add()
                        m_at = merged[:, bass.ds(i * (2 * PAIR) + j * PAIR, PAIR), :]
                        for ap in (m_at[:, :, 0:SEQ], m_at[:, :, SEQ:2 * SEQ]):
                            dve.lower_ap(ap)
                        wait(dve, (merged_hi, branch_pairs.now))
                        nc.vector.tensor_tensor(m_at[:, :, SEQ:2 * SEQ], part[:, j * PAIR:(j + 1) * PAIR, :],
                                                m_at[:, :, 0:SEQ], ALU.subtract).then_inc(merged_lo, 1)
                with loop(dve, OUT_ITERS, {split: 4, sets: 2, pair: 2}) as i:
                    lo()
                    lo()
                    lo()
                    for j in range(2):
                        t = i * (2 * PAIR) + j * PAIR
                        x_at = xt[:, at(t), :]
                        dve.lower_ap(x_at)
                        summed = sum_acc()
                        nc.vector.tensor_tensor(x_at, x_at, summed, ALU.add).then_inc(x_new, 1)
                        moving_x(t, cur[:, bass.ds(i * (2 * PAIR) + (P_FFN2 + j * PAIR), PAIR)])
                        if j == 0:
                            lo()
                ffn(P_NEXT)
            wait(dve, (msq_summed, norm.now + 1))
            nc.vector.tensor_scalar(out_ms[:, :], out_msq_ps, NORM_EPS, None, ALU.add).then_inc(msq_ready, 1)
            wait(dve, (inv_ready, norm.now + 1))
            refine(out_rstd[:, :], out_inv[:, :], out_ms[:, :])
            dve.sem_inc(out_rstd_ready, 1)

        @block.tensor
        def _(pe):
            unit = Count()
            sets = Count()
            norm = Count()
            pairs = Count()
            hidden = Count()
            head = Count()
            layers = Count()
            mixes = Count()
            branch_pairs = Count()
            slot = [0]

            def multiply(s, x_tiles, first, last, *needs):
                r = slot[0] % RING
                wait(pe, *needs, (hi_split, unit.now + 1), (lo_split, unit.now + 1 + RING))
                for k, x in enumerate(x_tiles):
                    for m in range(PAIR):
                        cols = slice(m * P, (m + 1) * P)
                        end = last and k == len(x_tiles) - 1
                        nc.tensor.matmul(acc[s][:, m, :], w_hi[:, r, k, cols], x[:, 0:2 * SEQ],
                                         start=first and k == 0, stop=False, skip_group_check=True)
                        mm = nc.tensor.matmul(acc[s][:, m, 0:SEQ], w_lo[:, r, k, cols], x[:, 0:SEQ],
                                              start=False, stop=end, skip_group_check=True)
                mm.then_inc(used, 1)
                unit.add()
                slot[0] += 1

            def new_set():
                s = sets.fixed % ACCS
                sets.add()
                wait(pe, (acc_summed, sets.now))
                return s

            def two_sets(tiles, made, count, between=None):
                for n in range(KT // UK):
                    missing = (KT // UK - 1 - n) * UK // PAIR
                    if n and between:
                        between()
                    for j in range(2):
                        if n == 0:
                            s = new_set()
                        else:
                            s = (sets.fixed - 2 + j) % ACCS
                        multiply(s, [tiles[:, n * UK + k, :] for k in range(UK)], n == 0, n == KT // UK - 1,
                                 (made, count.now - missing))

            def mean_square():
                wait(pe, (square_added, pairs.now), (bias_copied, 1))
                for m in range(PAIR):
                    mm = nc.tensor.matmul(msq_ps, mean_ones[:, :], square_sum[:, m, :], start=(m == 0),
                                          stop=(m == PAIR - 1))
                mm.then_inc(msq_summed, 1)
                norm.add()

            def normed_sets(iterations):
                two_sets(xm, xm_lo, pairs, mean_square)
                with loop(pe, iterations, {unit: 4, sets: 2}, 1):
                    two_sets(xm, xm_lo, pairs)

            def ffn():
                normed_sets(GU_ITERS)
                hidden.add(GU_ITERS)
                with loop(pe, DOWN_ITERS, {unit: 12, sets: 2}):
                    for _ in range(2):
                        s = new_set()
                        for n in range(DOWN_UNITS):
                            tiles = range(n * UK, min((n + 1) * UK, FT))
                            multiply(s, [hm[:, k, :] for k in tiles], n == 0, n == DOWN_UNITS - 1,
                                     (hid_lo, hidden.now - (FT - 1 - tiles[-1]) // PAIR))
                pairs.add(XPAIRS)

            pe.wait_ge(ones_ready, 2)
            pe.wait_ge(lam_summed, 1)
            nc.tensor.matmul(lam_ps, ones[0:1, :], lam_sum[0:1, :], start=True, stop=True).then_inc(lam_spread, 1)
            pe.wait_ge(ident_ready, 1)
            pe.wait_ge(lam_exped, 1)
            for b in range(XPAIRS):
                pe.wait_ge(x_loaded[b // 2], 16)
                for k in range(2):
                    for t in range(QT):
                        col = (k * QT + t) * P
                        kt = 2 * b + k
                        mm = nc.tensor.transpose(acc[b // 2][:, b % 2, col:col + P],
                                                 x_tok[:, t, kt * P:(kt + 1) * P], ident[:, :])
                mm.then_inc(x_turned, 1)
            pairs.add(XPAIRS)
            pe.wait_ge(table_ready, 1)
            pe.wait_ge(onehot_ready, 1)
            for h in range(N_HEADS):
                for n, part_of in enumerate((table_hi, table_lo)):
                    mm = nc.tensor.matmul(side[h][:, 0:BIAS_LEN], part_of[0:NUM_BUCKETS, h, :],
                                          onehot_r[0:NUM_BUCKETS, :], start=n == 0, stop=n == 1)
            mm.then_inc(bias_spread, 1)
            pe.wait_ge(x_new, XPAIRS)
            with loop(pe, DEPTH, {unit: UNITS_LAYER, sets: SETS_LAYER, norm: NORMS_LAYER, pairs: 3 * XPAIRS,
                                  hidden: 2 * GU_ITERS, head: N_HEADS, layers: 1,
                                  branch_pairs: XPAIRS, mixes: 3}):
                ffn()
                normed_sets(QKV_ITERS)

                def first_unit():
                    multiply(new_set(), [xm[:, k, :] for k in range(UK)], True, False)

                def second_set_started():
                    multiply(new_set(), [xm[:, k, :] for k in range(UK)], True, False)

                def both_finished():
                    for j in range(2):
                        multiply((sets.fixed - 2 + j) % ACCS, [xm[:, k, :] for k in range(UK, KT)], False, True)

                first_unit()
                with loop(pe, HEAD_ITERS, {unit: 4, sets: 2, head: 1}):
                    head.add()
                    wait(pe, (head_copied, head.now + layers.now))
                    for sm in range(2):
                        half = slice(sm * HEAD_DIM, (sm + 1) * HEAD_DIM)
                        nc.tensor.matmul(score[:, sm, 0:SEQ], head_qkv[half, 0, P:SEQ], head_qkv[half, 1, :],
                                         start=True, stop=True)
                        mm = nc.tensor.matmul(score[:, sm, SEQ:KEYS], head_qkv[half, 0, 0:P],
                                              head_qkv[half, 1, 0:P], start=True, stop=True)
                    mm.then_inc(scored, 1)
                    wait(pe, (pv_read, head.now))
                    for t in range(QT):
                        mm = nc.tensor.transpose(v_ps[:, t * V_DIM:(t + 1) * V_DIM],
                                                 head_qkv[:, 2, t * P:(t + 1) * P], ident[:, :])
                    mm.then_inc(v_turned, 1)
                    second_set_started()
                    both_finished()
                    wait(pe, (prob_ready, head.now))
                    for b in range(KEYS // P):
                        mm = nc.tensor.transpose(prob_t_ps[:, b * P:(b + 1) * P], prob[:, b * P:(b + 1) * P],
                                                 ident[:, :])
                    mm.then_inc(prob_turned, 1)
                    first_unit()
                    wait(pe, (v_copied, head.now), (prob_copied, head.now))
                    for k in range(QT):
                        nc.tensor.matmul(pv_ps[:, 1, :], prob_t[:, k * P:(k + 1) * P], v_tok[:, k, :],
                                         start=(k == 0), stop=(k == QT - 1))
                    nc.tensor.matmul(pv_ps[:, 0, :], prob_t[:, SEQ:KEYS], v_tok[:, 0, :], start=True,
                                     stop=True).then_inc(pv_done, 1)
                with loop(pe, UC_ITERS, {unit: 4, sets: 2}):
                    second_set_started()
                    both_finished()
                    first_unit()
                layers.add()
                second_set_started()
                wait(pe, (attn_scaled, layers.now))
                for h in range(N_HEADS):
                    for t in range(QT):
                        col = ((h % 2) * QT + t) * P
                        mm = nc.tensor.transpose(side[h // 2][:, col:col + P], attn[:, h, t, :], ident[:, :])
                mm.then_inc(attn_turned, 1)
                both_finished()
                mixes.add(3)
                with loop(pe, BRANCH_ITERS, {unit: 4, sets: 4}):
                    for n in range(2):
                        for j in range(2):
                            multiply(new_set(), [mix[:, n * UK + k, :] for k in range(UK)], True, True,
                                     (mix_lo, mixes.now - 2 + 2 * n))
                branch_pairs.add(XPAIRS)
                with loop(pe, OUT_ITERS, {unit: 4, sets: 2}):
                    two_sets(merged, merged_lo, branch_pairs)
                pairs.add(XPAIRS)
                ffn()
            for b in range(XPAIRS):
                pe.wait_ge(xg_ready, pairs.now - (XPAIRS - 1 - b))
                for k in range(2):
                    for t in range(QT):
                        col = (k * QT + t) * P
                        mm = nc.tensor.transpose(side[b][:, col:col + P], xg[:, 2 * b + k, t * P:(t + 1) * P],
                                                 ident[:, :])
                mm.then_inc(y_turned, 1)
            wait(pe, (square_added, pairs.now))
            for t in range(QT):
                for m in range(PAIR):
                    mm = nc.tensor.matmul(out_msq_ps[:, t:t + 1], square_sum[:, m, t * P:(t + 1) * P],
                                          mean_ones[:, 0:1], start=(m == 0), stop=(m == PAIR - 1))
            mm.then_inc(msq_summed, 1)


_INS = ["x", "norm_ffn1_g", "ffn1_w_gate", "ffn1_w_up", "ffn1_w_down", "norm_mix_g", "w_in", "lambda_q1",
        "lambda_k1", "lambda_q2", "lambda_k2", "subln_g", "rel_bias", "conv_w", "w_branch_attn",
        "w_branch_conv", "w_out", "norm_ffn2_g", "ffn2_w_gate", "ffn2_w_up", "ffn2_w_down", "final_g"]


def kernel(**inputs):
    import numpy as _np
    import concourse.bacc as _bacc
    from concourse import mybir as _mybir
    from concourse.bass_utils import run_bass_kernel_spmd as _run

    nc = _bacc.Bacc("TRN2", target_bir_lowering=False, num_devices=1)
    arrays, args = {}, []
    for name in _INS + ["places"]:
        a = bucket_places() if name == "places" else _np.ascontiguousarray(inputs[name])
        arrays[f"in_{name}_dram"] = a
        args.append(nc.dram_tensor(f"in_{name}_dram", a.shape, _mybir.dt.from_np(a.dtype), kind="ExternalInput").ap())
    out = nc.dram_tensor("out_0_dram", (1, SEQ, D_MODEL), F32, kind="ExternalOutput").ap()
    trunk(nc, *args, out)
    r = _run(nc, [arrays], core_ids=[0])
    return r.results[0]["out_0_dram"]
```

```python
import math
from contextlib import ExitStack, contextmanager

import numpy as np

import concourse.bass as bass
from concourse import mybir

F32 = mybir.dt.float32
F32R = mybir.dt.float32r
ACT = mybir.ActivationFunctionType
ALU = mybir.AluOpType
AX = mybir.AxisListType

P = 128
D_MODEL, SEQ, DEPTH = 1024, 256, 2
HEAD_DIM = 64
V_DIM = 2 * HEAD_DIM
ATTN_W = D_MODEL // 2
N_HEADS = ATTN_W // V_DIM
QK_W = N_HEADS * 2 * HEAD_DIM
CONV_W = D_MODEL // 2
CONV_K = 3
D_FF = (((8 * D_MODEL) // 3 + 255) // 256) * 256
NUM_BUCKETS = 32
MAX_EXACT = NUM_BUCKETS // 2
MAX_DISTANCE = 128
NORM_EPS = 1e-6
SUBLN_EPS = 1e-5
MASKED = -1.0e30

KT = D_MODEL // P
FT = D_FF // P
QT = SEQ // P
PAIR = 2
COLS = PAIR * P
UK = 4
RING = 4
LEAD = 3
ACCS = 2

IN_COLS = 2 * QK_W + ATTN_W + 3 * CONV_W + 2 * D_MODEL

GU_ITERS = FT // PAIR
DOWN_UNITS = -(-FT // UK)
DOWN_ITERS = KT // PAIR // 2
QKV_ITERS = (2 * QK_W + ATTN_W) // (2 * COLS)
CONV_T = CONV_W // P
HEAD_ITERS = N_HEADS
GATE_ITERS = IN_COLS // (2 * COLS) - QKV_ITERS - HEAD_ITERS
BRANCH_ITERS = KT // PAIR // 2
OUT_ITERS = KT // PAIR // 2

GU_UNITS = 4
DOWN_BODY = 2 * DOWN_UNITS
UNITS_LAYER = (2 * (GU_ITERS * GU_UNITS + DOWN_ITERS * DOWN_BODY)
               + 4 * (QKV_ITERS + HEAD_ITERS + GATE_ITERS + BRANCH_ITERS + OUT_ITERS))
SETS_LAYER = 2 * 2 * (GU_ITERS + DOWN_ITERS) + 2 * (QKV_ITERS + HEAD_ITERS + GATE_ITERS) \
    + 4 * BRANCH_ITERS + 2 * OUT_ITERS
COPIES_LAYER = SETS_LAYER - 4 * BRANCH_ITERS - 2 * OUT_ITERS
XPAIRS = KT // PAIR
NORMS_LAYER = 3
HEAD_STEPS = 6
STEPS_LAYER = 46

BIAS_ZERO = SEQ - 1
BIAS_LEN = SEQ + P
P_MIX, P_FFN2, P_NEXT, P_CONV, P_SUBLN, P_LAM = 0, KT, 2 * KT, 3 * KT, 3 * KT + CONV_K * CONV_T, \
    3 * KT + CONV_K * CONV_T + 1
PARS = P_LAM + 1


def lambda_init(layer):
    return 0.8 - 0.6 * math.exp(-0.3 * layer)


def bucket_places():
    n = np.arange(SEQ, dtype=np.int32)
    nf = np.maximum(n, MAX_EXACT).astype(np.float32)
    large = MAX_EXACT + (np.log(nf / np.float32(MAX_EXACT)) / np.float32(math.log(MAX_DISTANCE / MAX_EXACT))
                         * np.float32(NUM_BUCKETS - MAX_EXACT)).astype(np.int32)
    bucket = np.where(n < MAX_EXACT, n, np.minimum(large, NUM_BUCKETS - 1))
    places = np.zeros((NUM_BUCKETS, BIAS_LEN), np.float32)
    places[bucket, BIAS_ZERO - n] = 1.0
    return places


def at(t):
    return slice(t, t + PAIR) if isinstance(t, int) else bass.ds(t, PAIR)


class Count:

    def __init__(self, start=0):
        self.fixed, self.moving = start, 0

    def add(self, n=1):
        self.fixed += n
        return self.now

    @property
    def now(self):
        return self.moving + self.fixed


@contextmanager
def loop(eng, n, per, first=0):
    with eng.Fori(first, n) as i:
        before = {c: (c.fixed - first * step, c.moving) for c, step in per.items()}
        for c, step in per.items():
            c.fixed, c.moving = c.fixed - first * step, c.moving + i * step
        yield i
        for c, step in per.items():
            fixed, moving = before[c]
            assert c.fixed - fixed == step, (c.fixed - fixed, step)
            c.fixed, c.moving = fixed + n * step, moving


def wait(eng, *pairs):
    for _, value in pairs:
        if not isinstance(value, int):
            eng.compute_val(value)
    for sem, value in pairs:
        eng.wait_ge(sem, value)


def trunk(nc, x, norm_ffn1_g, ffn1_w_gate, ffn1_w_up, ffn1_w_down, norm_mix_g, w_in,
          lambda_q1, lambda_k1, lambda_q2, lambda_k2, subln_g, rel_bias, conv_w,
          w_branch_attn, w_branch_conv, w_out, norm_ffn2_g, ffn2_w_gate, ffn2_w_up,
          ffn2_w_down, final_g, places, out):
    with ExitStack() as ctx:
        def sb(name, shape, dt=F32):
            return ctx.enter_context(nc.sbuf_tensor(name, [P, *shape], dt))

        def psum(name, shape):
            return ctx.enter_context(nc.psum_tensor(name, [P, *shape], F32))

        def sem(name):
            return ctx.enter_context(nc.semaphore(name))

        raw = sb("raw", [RING, UK, COLS])
        w_hi = sb("w_hi", [RING, UK, COLS], F32R)
        w_lo = sb("w_lo", [RING, UK, COLS], F32R)
        xt = sb("xt", [KT, SEQ])
        xm = sb("xm", [KT, 2 * SEQ], F32R)
        hm = sb("hm", [FT, 2 * SEQ], F32R)
        merged = hm[:, 0:KT, :]
        mix = hm[:, KT:2 * KT, :]
        proj = sb("proj", [3 * N_HEADS + 1, SEQ])
        late = sb("late", [3 * CONV_T + 2 * KT, SEQ])
        conv_b, conv, conv_in = (late[:, n * CONV_T:(n + 1) * CONV_T, :] for n in range(3))
        gates = late[:, 3 * CONV_T:, :]
        xg = late[:, 0:KT, :]
        x_tok = gates[:, 0:KT, :].rearrange("p k n -> p (k n)").rearrange("p (t d) -> p t d", t=QT)
        y_tok = gates[:, KT:2 * KT, :].rearrange("p k n -> p (k n)").rearrange("p (t d) -> p t d", t=QT)
        bias = sb("bias", [N_HEADS, SEQ + P])
        acc_lo = [sb(f"acc_lo{s}", [PAIR, SEQ]) for s in range(ACCS)]
        sums = [sb(f"sum{s}", [PAIR, SEQ]) for s in range(ACCS)]
        ffn_store = sb("ffn_store", [2 * PAIR, SEQ])
        silu, hid = ffn_store[:, 0:PAIR, :], ffn_store[:, PAIR:, :]
        part = sb("part", [2 * PAIR, SEQ])
        square = sb("square", [PAIR, SEQ])
        square_sum = sb("square_sum", [PAIR, SEQ])
        mean_sq = sb("mean_sq", [SEQ])
        newton = sb("newton", [SEQ])
        inv = sb("inv", [SEQ])
        rstd = sb("rstd", [SEQ])
        half_rstd = sb("half_rstd", [SEQ])
        out_ms, out_inv, out_rstd = (sb(n, [QT]) for n in ("out_ms", "out_inv", "out_rstd"))
        KEYS = SEQ + P
        head_qkv = sb("head_qkv", [3, SEQ])
        logits, expo = (v[:, :, :].rearrange("p k n -> p (k n)")[:, 0:2 * KEYS].rearrange(
            "p (s k) -> p s k", s=2) for v in (ffn_store, part))
        prob = sb("prob", [KEYS])
        row_max = sb("row_max", [QT, 2])
        neg_max = sb("neg_max", [QT, 2])
        row_sum = sb("row_sum", [QT, 2])
        row_inv = sb("row_inv", [QT, 2])
        lam_inv = sb("lam_inv", [QT])
        prob_t = sb("prob_t", [KEYS])
        v_tok = sb("v_tok", [QT, V_DIM])
        attn = sb("attn", [N_HEADS, QT, V_DIM])
        attn_sq = sb("attn_sq", [N_HEADS * QT])
        attn_ms = sb("attn_ms", [N_HEADS * QT])
        attn_inv = sb("attn_inv", [N_HEADS * QT])
        attn_rstd = sb("attn_rstd", [N_HEADS * QT])
        ident = sb("ident", [P])
        mean_ones = sb("mean_ones", [P])
        pars = sb("pars", [DEPTH, PARS])
        cur = sb("cur", [PARS])
        first_g = sb("first_g", [KT])
        eps = sb("eps", [1])
        table_probe = sb("table_probe", [4])
        lam_rows = sb("lam_rows", [4, DEPTH * HEAD_DIM])
        lam_prod = sb("lam_prod", [2, DEPTH * HEAD_DIM])
        lam_scratch = sb("lam_scratch", [2, DEPTH * HEAD_DIM])
        lam_sum = sb("lam_sum", [2 * DEPTH])
        lam_exp = sb("lam_exp", [2, DEPTH])
        lam_diff = sb("lam_diff", [DEPTH])
        table = sb("table", [N_HEADS])
        onehot = part[:, 0:PAIR, :].rearrange("p k n -> p (k n)")[:, 0:BIAS_LEN]
        table_hi = hm[:, 0, :].rearrange("p (h m) -> p h m", h=N_HEADS)
        table_lo = hm[:, 1, :].rearrange("p (h m) -> p h m", h=N_HEADS)
        onehot_r = hm[:, 2, 0:BIAS_LEN]
        bias_rows = proj[:, 0:2 * N_HEADS, :].rearrange("p k n -> p (k n)")[:, 0:N_HEADS * BIAS_LEN] \
            .rearrange("p (h m) -> p h m", h=N_HEADS)
        bias_dram = nc.dram_tensor("bias_scratch", (N_HEADS, P * BIAS_LEN), F32, kind="Internal").ap()

        acc = [psum(f"acc{s}", [PAIR, 2 * SEQ]) for s in range(ACCS)]
        score = psum("score", [2, 2 * SEQ])
        mixed = psum("mixed", [2, 2 * SEQ])
        ps_c, ps_d = mixed[:, 0, :], mixed[:, 1, :]
        merge_sets = [score, mixed, acc[0], acc[1]]
        side = [score[:, 0, :], score[:, 1, :], ps_c, ps_d]
        prob_t_ps = ps_c[:, 0:KEYS]
        v_ps = ps_d[:, 0:QT * V_DIM]
        pv_ps = ps_d[:, SEQ:SEQ + QT * V_DIM].rearrange("p (t d) -> p t d", t=QT)
        msq_ps = ps_c[:, 0:SEQ]
        out_msq_ps = acc[0][:, 0, 0:QT]

        loaded = [sem(f"loaded{s}") for s in range(RING)]
        x_loaded = [sem(f"x_loaded{b}") for b in range(2)]
        gain_loaded, pars_loaded, lam_loaded, table_loaded = (sem(n) for n in (
            "gain_loaded", "pars_loaded", "lam_loaded", "table_loaded"))
        bias_stored, bias_loaded, out_stored = sem("bias_stored"), sem("bias_loaded"), sem("out_stored")
        hi_split = sem("hi_split")
        lo_split = sem("lo_split")
        used = sem("used")
        acc_copied = sem("acc_copied")
        acc_summed = sem("acc_summed")
        gate_ready, silu_done, hid_ready, hid_hi, hid_lo = (sem(n) for n in (
            "gate_ready", "silu_done", "hid_ready", "hid_hi", "hid_lo"))
        x_new, squared, square_added, xg_ready, xm_hi, xm_lo = (sem(n) for n in (
            "x_new", "squared", "square_added", "xg_ready", "xm_hi", "xm_lo"))
        msq_summed, msq_ready, inv_ready = (sem(n) for n in ("msq_summed", "msq_ready", "inv_ready"))
        scored, max_ready, exp_done, prob_ready, prob_turned, prob_copied = (sem(n) for n in (
            "scored", "max_ready", "exp_done", "prob_ready", "prob_turned", "prob_copied"))
        proj_ready, head_copied = sem("proj_ready"), sem("head_copied")
        v_turned, v_copied, pv_done, pv_read = (sem(n) for n in ("v_turned", "v_copied", "pv_done", "pv_read"))
        attn_squared, attn_rstd_ready = sem("attn_squared"), sem("attn_rstd_ready")
        conv_in_ready, conv_started = sem("conv_in_ready"), sem("conv_started")
        out_rstd_ready, pars_ready, onehot_ready = (sem(n) for n in ("out_rstd_ready", "pars_ready", "onehot_ready"))
        attn_ms_ready, attn_inv_ready, attn_scaled, attn_turned, attn_gained, attn_hi = (sem(n) for n in (
            "attn_ms_ready", "attn_inv_ready", "attn_scaled", "attn_turned", "attn_gained", "attn_hi"))
        mix_lo, conv_ready, conv_hi = sem("mix_lo"), sem("conv_ready"), sem("conv_hi")
        gates_done, merged_ready, merged_hi, merged_lo = (sem(n) for n in (
            "gates_done", "merged_ready", "merged_hi", "merged_lo"))
        vec_step = sem("vec_step")
        ident_zeroed, ident_ready, ones_ready = sem("ident_zeroed"), sem("ident_ready"), sem("ones_ready")
        x_turned, lam_multiplied, lam_summed, lam_exped = (sem(n) for n in (
            "x_turned", "lam_multiplied", "lam_summed", "lam_exped"))
        table_ready, bias_spread, bias_rows_ready = sem("table_ready"), sem("bias_spread"), sem("bias_rows_ready")
        bias_copied, lam_diffed = sem("bias_copied"), sem("lam_diffed")
        y_turned = sem("y_turned")
        y_copied = [sem(f"y_copied{e}") for e in range(2)]

        def wide(v):
            return v.unsqueeze(1).to_broadcast([P, PAIR, SEQ])

        def columns(v):
            return v.rearrange("(k p) -> p k", p=P)

        def y_at(b, t):
            return y_tok[:, t, b * COLS:(b + 1) * COLS].rearrange("p (k d) -> p k d", k=PAIR)

        def turned_at(b, t):
            return side[b].rearrange("p (k t d) -> p k t d", k=PAIR, t=QT)[:, :, t]

        block = ctx.enter_context(nc.Block())

        @block.sync
        def _(sp):
            split = Count(1)
            slot = [0]

            def load(src):
                s = slot[0] % RING
                sp.lower_ap_dma(src)
                wait(sp, (lo_split, split.now))
                sp.dma_start(raw[:, s, 0:src.shape[1], :], src).then_inc(loaded[s], 16)
                split.add()
                slot[0] += 1

            def rows(w, l):
                return w[bass.ds(l, 1)].rearrange("o (k p) n -> p (o k) n", p=P)

            def full(w, l, col):
                for k in range(0, KT, UK):
                    load(rows(w, l)[:, k:k + UK, bass.ds(col, COLS)])

            def two_sets(l, wa, a, wb, b, in_turn=False):
                if not in_turn:
                    full(wa, l, a)
                    full(wb, l, b)
                    return
                for k in range(0, KT, UK):
                    load(rows(wa, l)[:, k:k + UK, bass.ds(a, COLS)])
                    load(rows(wb, l)[:, k:k + UK, bass.ds(b, COLS)])

            def down(w, l, col):
                for k in range(0, FT, UK):
                    load(rows(w, l)[:, k:min(k + UK, FT), bass.ds(col, COLS)])

            for b in range(2):
                half = slice(b * D_MODEL // 2, (b + 1) * D_MODEL // 2)
                sp.dma_start(x_tok[:, :, half],
                             x[0].rearrange("(t p) d -> p t d", p=P)[:, :, half]).then_inc(x_loaded[b], 16)

            with loop(sp, DEPTH, {split: UNITS_LAYER}) as l:
                two_sets(l, ffn1_w_gate, 0, ffn1_w_up, 0, in_turn=True)
                with loop(sp, GU_ITERS, {split: GU_UNITS}, 1) as i:
                    two_sets(l, ffn1_w_gate, i * COLS, ffn1_w_up, i * COLS)
                with loop(sp, DOWN_ITERS, {split: DOWN_BODY}) as i:
                    for j in range(2):
                        down(ffn1_w_down, l, i * (2 * COLS) + j * COLS)
                two_sets(l, w_in, 0, w_in, COLS, in_turn=True)
                with loop(sp, IN_COLS // (2 * COLS), {split: 4}, 1) as i:
                    two_sets(l, w_in, i * (2 * COLS), w_in, i * (2 * COLS) + COLS)
                with loop(sp, BRANCH_ITERS, {split: 4}) as i:
                    for w in (w_branch_attn, w_branch_conv):
                        for j in range(2):
                            load(rows(w, l)[:, :, bass.ds(i * (2 * COLS) + j * COLS, COLS)])
                for i in range(OUT_ITERS):
                    two_sets(l, w_out, i * (2 * COLS), w_out, i * (2 * COLS) + COLS, in_turn=i == 0)
                two_sets(l, ffn2_w_gate, 0, ffn2_w_up, 0, in_turn=True)
                with loop(sp, GU_ITERS, {split: GU_UNITS}, 1) as i:
                    two_sets(l, ffn2_w_gate, i * COLS, ffn2_w_up, i * COLS)
                with loop(sp, DOWN_ITERS, {split: DOWN_BODY}) as i:
                    for j in range(2):
                        down(ffn2_w_down, l, i * (2 * COLS) + j * COLS)
            for n in range(LEAD):
                wait(sp, (lo_split, split.now + n))
                sp.sem_inc(loaded[n], 16)

            for b in (0, 2, 1, 3):
                sp.wait_ge(y_copied[b // 2], b % 2 + 1)
                sp.dma_start(out[0].rearrange("(t p) d -> p t d", p=P)[:, :, b * COLS:(b + 1) * COLS],
                             y_tok[:, :, b * COLS:(b + 1) * COLS]).then_inc(out_stored, 16)
            sp.wait_ge(out_stored, 16 * XPAIRS)

        @block.gpsimd
        def _(pool):
            nc.gpsimd.memset(ident[:, :], 0.0).then_inc(ident_zeroed, 1)
            nc.gpsimd.memset(mean_ones[:, :], 1.0 / D_MODEL).then_inc(ones_ready, 1)
            pool.wait_ge(ident_zeroed, 1)
            nc.gpsimd.affine_select(out=ident[:, :], in_=ident[:, :], compare_op=ALU.not_equal, fill=1.0,
                                    base=0, pattern=[[-1, P]], channel_multiplier=1).then_inc(ident_ready, 1)
            nc.gpsimd.memset(proj[:, 3 * N_HEADS, :], 0.0).then_inc(ones_ready, 1)
            nc.gpsimd.memset(eps[:, :], SUBLN_EPS).then_inc(ones_ready, 1)
            for n, v in enumerate((lambda_q1, lambda_k1, lambda_q2, lambda_k2)):
                pool.dma_start(lam_rows[:, n, :], v.rearrange("(o l) d -> o (l d)", o=1).to_broadcast(
                    [P, DEPTH * HEAD_DIM])).then_inc(lam_loaded, 16)
            pool.wait_ge(lam_loaded, 64)
            for s in range(2):
                last = nc.gpsimd.tensor_tensor(lam_prod[:, s, :], lam_rows[:, 2 * s, :], lam_rows[:, 2 * s + 1, :],
                                               ALU.mult)
            last.then_inc(lam_multiplied, 1)
            def par(l, at, src):
                pool.dma_start(pars[:, l, at:at + src.shape[1]], src,
                               allow_slow_non_contiguous=True).then_inc(pars_loaded, 16)

            for l in range(DEPTH):
                par(l, P_MIX, columns(norm_mix_g[l]))
                par(l, P_FFN2, columns(norm_ffn2_g[l]))
                par(l, P_NEXT, columns(norm_ffn1_g[l + 1] if l + 1 < DEPTH else final_g))
                par(l, P_SUBLN, columns(subln_g[l]))
                for k in range(CONV_K):
                    par(l, P_CONV + k * CONV_T, columns(conv_w[l, k]))
            pool.wait_ge(bias_copied, 1)
            nc.gpsimd.memset(bias_rows[:, :, BIAS_ZERO + 1:], MASKED).then_inc(bias_rows_ready, 1)
            pool.wait_ge(bias_rows_ready, 1)
            pool.dma_start(bias_dram.rearrange("h (p m) -> p h m", p=P), bias_rows).then_inc(bias_stored, 16)
            pool.wait_ge(bias_stored, 16)
            back = bias_dram[:, P - 1:P - 1 + P * (BIAS_LEN - 1)].rearrange("h (p m) -> p h m", p=P)
            pool.dma_start(bias[:, :, 0:SEQ], back[:, :, 0:SEQ]).then_inc(bias_loaded, 16)
            pool.dma_start(bias[:, :, SEQ:], back[:, :, P:SEQ]).then_inc(bias_loaded, 16)
            pool.wait_ge(lam_exped, 1)
            nc.gpsimd.tensor_tensor(lam_diff[:, :], lam_exp[:, 0, :], lam_exp[:, 1, :],
                                    ALU.subtract).then_inc(lam_diffed, 1)
            pool.wait_ge(lam_diffed, 1)
            pool.wait_ge(pars_loaded, 16 * DEPTH * (4 + CONV_K))
            for l in range(DEPTH):
                nc.gpsimd.tensor_scalar(pars[:, l, P_LAM:P_LAM + 1], lam_diff[:, l:l + 1], lambda_init(l),
                                        None, ALU.add)
                nc.gpsimd.tensor_scalar(pars[:, l, P_SUBLN:P_SUBLN + 1], pars[:, l, P_SUBLN:P_SUBLN + 1],
                                        1.0 - lambda_init(l), None, ALU.mult).then_inc(pars_ready, 1)
            pool.wait_ge(bias_loaded, 32)

        @block.scalar
        def _(act):
            split = Count()
            loads = Count()
            sets = Count()
            pair = Count()
            norm = Count()
            hidden = Count()
            head = Count()
            projs = Count()
            layers = Count()
            branch_pairs = Count()
            probes = Count()
            spare = act.alloc_register("spare")
            slot = [0]
            units_done = Count(RING)

            def hi(tiles=UK):
                s = slot[0] % RING
                wait(act, (loaded[s], loads.now + 16), (used, split.now + 1))
                nc.scalar.copy(w_hi[:, s, 0:tiles, :], raw[:, s, 0:tiles, :]).then_inc(hi_split, 1)
                split.add()
                slot[0] += 1
                if slot[0] % RING == 0:
                    loads.add(16)

            def copy_acc(units):
                s = sets.fixed % ACCS
                units_done.add(units)
                wait(act, (used, units_done.now), (acc_summed, sets.now + 1))
                nc.scalar.copy(acc_lo[s][:, :, :], acc[s][:, :, SEQ:2 * SEQ]).then_inc(acc_copied, 1)
                sets.add()

            def moving_x(t, moving):
                pair.add()
                wait(act, (x_new, pair.now))
                if moving:
                    act.reg_mov(spare, 0)
                nc.scalar.activation(square[:, :, :], xt[:, at(t), :], ACT.Square).then_inc(squared, 1)
                wait(act, (xg_ready, pair.now))
                if moving:
                    act.reg_mov(spare, 0)
                nc.scalar.copy(xm[:, at(t), 0:SEQ], xg[:, at(t), :]).then_inc(xm_hi, 1)

            def norm_root():
                norm.add()
                wait(act, (msq_ready, norm.now))
                nc.scalar.activation(inv[:, :], mean_sq[:, :], ACT.Abs_reciprocal_sqrt).then_inc(inv_ready, 1)

            def have_table(function):
                nc.scalar.activation(table_probe[:, probes.now:probes.now + 1], eps[:, :], function)
                probes.add()

            def two_sets(between=None):
                hi()
                hi()
                if between:
                    hi()
                    between()
                copy_acc(3 if between else 2)
                hi()
                if not between:
                    hi()
                copy_acc(1 if between else 2)

            def ffn():
                def gate_up(i, first):
                    hi()
                    hi()
                    if first:
                        hi()
                        norm_root()
                    copy_acc(3 if first else 2)
                    hi()
                    hidden.add()
                    wait(act, (gate_ready, hidden.now))
                    nc.scalar.activation(silu[:, :, :], sums[0][:, :, :], ACT.Silu).then_inc(silu_done, 1)
                    if not first:
                        hi()
                    copy_acc(1 if first else 2)
                    wait(act, (hid_ready, hidden.now))
                    if not first:
                        act.reg_mov(spare, 0)
                    nc.scalar.copy(hm[:, at(i * PAIR), 0:SEQ], hid[:, :, :]).then_inc(hid_hi, 1)

                gate_up(0, True)
                with loop(act, GU_ITERS, {split: 4, loads: 16, sets: 2, units_done: 4, hidden: 1}, 1) as i:
                    gate_up(i, False)
                with loop(act, DOWN_ITERS, {split: 12, loads: 48, sets: 2, units_done: 12, pair: 2}) as i:
                    for j in range(2):
                        for k in range(DOWN_UNITS):
                            u = k + LEAD
                            hi(FT - UK * (DOWN_UNITS - 1) if u == DOWN_UNITS - 1 else UK)
                        copy_acc(DOWN_UNITS)
                        moving_x(i * (2 * PAIR) + j * PAIR, True)

            act.dma_start(first_g[:, :], columns(norm_ffn1_g[0]), allow_slow_non_contiguous=True) \
                .then_inc(gain_loaded, 16)
            act.dma_start(table[0:NUM_BUCKETS, :], rel_bias).then_inc(table_loaded, 16)
            act.dma_start(onehot[0:NUM_BUCKETS, :], places).then_inc(table_loaded, 16)
            squares = (square_sum, square, acc_lo[0], acc_lo[1])
            for first in range(0, XPAIRS, 2):
                for p in (first, first + 1):
                    act.wait_ge(x_turned, p + 1)
                    nc.scalar.copy(xt[:, 2 * p:2 * p + 2, :].rearrange("p k n -> p (k n)"),
                                   acc[p // 2][:, p % 2, :]).then_inc(x_new, 1)
                if not first:
                    act.wait_ge(table_loaded, 32)
                    nc.scalar.copy(onehot_r[0:NUM_BUCKETS, :], onehot[0:NUM_BUCKETS, :]).then_inc(onehot_ready, 1)
                for p in (first, first + 1):
                    act.wait_ge(xg_ready, p + 1)
                    nc.scalar.copy(xm[:, at(p * PAIR), 0:SEQ], xg[:, at(p * PAIR), :]).then_inc(xm_hi, 1)
                hi()
                if first:
                    hi()
                for p in (first, first + 1):
                    act.wait_ge(x_new, p + 1)
                    nc.scalar.activation(squares[p][:, :, :], xt[:, at(p * PAIR), :],
                                         ACT.Square).then_inc(squared, 1)
            pair.add(XPAIRS)
            act.wait_ge(bias_spread, 1)
            for h in range(N_HEADS):
                last = nc.scalar.copy(bias_rows[:, h, :], side[h][:, 0:BIAS_LEN])
            last.then_inc(bias_copied, 1)
            act.wait_ge(lam_multiplied, 1)
            for s in range(2):
                for l in range(DEPTH):
                    n = s * DEPTH + l
                    last = nc.scalar.activation(lam_scratch[:, s, l * HEAD_DIM:(l + 1) * HEAD_DIM],
                                                lam_prod[:, s, l * HEAD_DIM:(l + 1) * HEAD_DIM], ACT.Copy,
                                                accum_out=lam_sum[:, n:n + 1])
            last.then_inc(lam_summed, 1)
            act.wait_ge(lam_summed, 1)
            nc.scalar.activation(lam_exp[:, :, :], lam_sum[:, :].rearrange("p (s l) -> p s l", s=2),
                                 ACT.Exp).then_inc(lam_exped, 1)
            have_table(ACT.Silu)
            with loop(act, DEPTH, {split: UNITS_LAYER, loads: 4 * UNITS_LAYER, sets: SETS_LAYER,
                                   units_done: UNITS_LAYER, pair: 3 * XPAIRS, norm: NORMS_LAYER,
                                   hidden: 2 * GU_ITERS, head: N_HEADS, projs: 2 * QKV_ITERS, layers: 1,
                                   branch_pairs: XPAIRS}):
                ffn()
                two_sets(norm_root)
                with loop(act, QKV_ITERS, {split: 4, loads: 16, sets: 2, units_done: 4}, 1):
                    two_sets()
                projs.add(2 * QKV_ITERS)
                have_table(ACT.Exp)

                wait(act, (proj_ready, projs.now))
                nc.scalar.copy(head_qkv[:, :, :], proj[:, 0:3 * N_HEADS, :].rearrange(
                    "p (a h) n -> p h a n", a=3)[:, 0]).then_inc(head_copied, 1)
                with loop(act, HEAD_ITERS, {split: 4, loads: 16, sets: 2, units_done: 4, head: 1}) as h:
                    head.add()
                    hi()
                    hi()
                    wait(act, (v_turned, head.now))
                    nc.scalar.copy(v_tok[:, :, :].rearrange("p t d -> p (t d)"), v_ps).then_inc(v_copied, 1)
                    wait(act, (max_ready, head.now))
                    for t, (a, b) in enumerate(((SEQ, KEYS), (0, SEQ))):
                        for s in range(2):
                            last = nc.scalar.activation(expo[:, s, a:b], logits[:, s, a:b], ACT.Exp,
                                                        bias=neg_max[:, t, s:s + 1],
                                                        accum_out=row_sum[:, t, s:s + 1])
                    last.then_inc(exp_done, 1)
                    copy_acc(2)
                    hi()
                    hi()
                    copy_acc(2)
                    wait(act, (prob_turned, head.now))
                    nc.scalar.copy(prob_t[:, :], prob_t_ps).then_inc(prob_copied, 1)
                    nc.scalar.copy(head_qkv[:, :, :], proj[:, 1:3 * N_HEADS + 1, :].rearrange(
                        "p (a h) n -> p h a n", a=3)[:, bass.ds(h, 1)].rearrange(
                            "p o a n -> p (o a) n")).then_inc(head_copied, 1)
                    wait(act, (pv_done, head.now))
                    act.reg_mov(spare, 0)
                    nc.scalar.copy(attn[:, bass.ds(h, 1)].rearrange("p o t d -> p (o t) d"),
                                   pv_ps).then_inc(pv_read, 1)
                layers.add()
                hi()
                hi()
                copy_acc(2)
                wait(act, (pv_read, head.now + 1))
                for h in range(N_HEADS):
                    for t in range(QT):
                        n = h * QT + t
                        last = nc.scalar.activation(part[:, n // 2, (n % 2) * V_DIM:(n % 2 + 1) * V_DIM],
                                                    attn[:, h, t, :], ACT.Square, accum_out=attn_sq[:, n:n + 1])
                last.then_inc(attn_squared, 1)
                hi()
                hi()
                copy_acc(2)
                hi()
                wait(act, (conv_in_ready, layers.now))
                for t in range(CONV_T):
                    tap = P_CONV + (CONV_K - 1) * CONV_T + t
                    last = nc.scalar.activation(conv[:, t, :], conv_in[:, t, :], ACT.Copy, scale=cur[:, tap:tap + 1])
                last.then_inc(conv_started, 1)
                wait(act, (attn_ms_ready, layers.now))
                nc.scalar.activation(attn_inv[:, :], attn_ms[:, :],
                                     ACT.Abs_reciprocal_sqrt).then_inc(attn_inv_ready, 1)
                hi()
                copy_acc(2)
                hi()
                wait(act, (attn_rstd_ready, layers.now))
                for h in range(N_HEADS):
                    for t in range(QT):
                        n = h * QT + t
                        last = nc.scalar.activation(attn[:, h, t, :], attn[:, h, t, :], ACT.Copy,
                                                    scale=attn_rstd[:, n:n + 1])
                last.then_inc(attn_scaled, 1)
                hi()
                copy_acc(2)
                hi()
                wait(act, (attn_turned, layers.now))
                for b in range(2):
                    last = nc.scalar.activation(
                        attn[:, 2 * b:2 * b + 2].rearrange("p h t d -> p (h t d)"), side[b], ACT.Copy,
                        scale=cur[:, P_SUBLN:P_SUBLN + 1])
                last.then_inc(attn_gained, 1)
                hi()
                wait(act, (attn_gained, layers.now))
                nc.scalar.copy(mix[:, 0:N_HEADS, 0:SEQ],
                               attn[:, :, :, :].rearrange("p h t d -> p h (t d)")).then_inc(attn_hi, 1)
                copy_acc(2)
                hi()
                hi()
                wait(act, (conv_ready, layers.now))
                nc.scalar.copy(mix[:, N_HEADS:, 0:SEQ], conv).then_inc(conv_hi, 1)
                have_table(ACT.Sigmoid)
                copy_acc(2)
                sets.add(4 * BRANCH_ITERS + 2 * OUT_ITERS)
                units_done.add(4 * (BRANCH_ITERS + OUT_ITERS))
                with loop(act, BRANCH_ITERS, {split: 4, loads: 16, branch_pairs: 2}) as i:
                    for g in range(2):
                        hi()
                        g_at = gates[:, bass.ds(i * (2 * PAIR) + g * KT, 2 * PAIR), :]
                        nc.scalar.activation(g_at, g_at, ACT.Sigmoid).then_inc(gates_done, 1)
                        hi()
                    for j in range(2):
                        branch_pairs.add()
                        wait(act, (merged_ready, branch_pairs.now))
                        act.reg_mov(spare, 0)
                        nc.scalar.copy(merged[:, bass.ds(i * (2 * PAIR) + j * PAIR, PAIR), 0:SEQ],
                                       part[:, j * PAIR:(j + 1) * PAIR, :]).then_inc(merged_hi, 1)
                for i in range(OUT_ITERS):
                    for j in range(2):
                        for _ in range(2 if i else 3 - 2 * j):
                            hi()
                        moving_x((2 * i + j) * PAIR, False)
                ffn()
            wait(act, (msq_ready, norm.now + 1))
            nc.scalar.activation(out_inv[:, :], out_ms[:, :], ACT.Abs_reciprocal_sqrt).then_inc(inv_ready, 1)
            wait(act, (out_rstd_ready, 1))
            for b in range(2):
                act.wait_ge(y_turned, b + 1)
                for t in range(QT):
                    last = nc.scalar.activation(y_at(b, t), turned_at(b, t), ACT.Copy, scale=out_rstd[:, t:t + 1])
                last.then_inc(y_copied[0], 1)

        @block.vector
        def _(dve):
            split = Count()
            sets = Count()
            pair = Count()
            norm = Count()
            hidden = Count()
            head = Count()
            layers = Count()
            branch_pairs = Count()
            copies = Count()
            gated = Count()
            step = Count()
            slot = [0]

            def own(ins):
                ins.then_inc(vec_step, 1)
                step.add()
                wait(dve, (vec_step, step.now))

            def lo(tiles=UK):
                s = slot[0] % RING
                wait(dve, (hi_split, split.now + 1))
                nc.vector.tensor_tensor(w_lo[:, s, 0:tiles, :], raw[:, s, 0:tiles, :], w_hi[:, s, 0:tiles, :],
                                        ALU.subtract).then_inc(lo_split, 1)
                split.add()
                slot[0] += 1

            def sum_acc():
                s = sets.fixed % ACCS
                sets.add()
                copies.add()
                wait(dve, (acc_copied, copies.now))
                nc.vector.tensor_tensor(sums[s][:, :, :], acc[s][:, :, 0:SEQ], acc_lo[s][:, :, :],
                                        ALU.add).then_inc(acc_summed, 1)
                wait(dve, (acc_summed, sets.now + ACCS))
                return sums[s][:, :, :]

            def take(out, banks, by, op, last_unit):
                sets.add()
                wait(dve, (used, last_unit))
                nc.vector.tensor_tensor(out, banks[:, :, 0:SEQ], by, op).then_inc(acc_summed, 1)

            def taken():
                wait(dve, (acc_summed, sets.now + ACCS))

            def moving_x(t, gains):
                pair.add()
                x_at, g_at, m_at = (v[:, at(t), :] for v in (xt, xg, xm))
                gain = gains.unsqueeze(2).to_broadcast([P, PAIR, SEQ])
                for ap in (x_at, g_at, gain, m_at[:, :, 0:SEQ], m_at[:, :, SEQ:2 * SEQ]):
                    dve.lower_ap(ap)
                wait(dve, (x_new, pair.now))
                nc.vector.tensor_tensor(g_at, x_at, gain, ALU.mult).then_inc(xg_ready, 1)
                wait(dve, (squared, pair.now))
                nc.vector.tensor_tensor(square_sum[:, :, :], square_sum[:, :, :], square[:, :, :],
                                        ALU.add).then_inc(square_added, 1)
                wait(dve, (xm_hi, pair.now))
                nc.vector.tensor_tensor(m_at[:, :, SEQ:2 * SEQ], g_at, m_at[:, :, 0:SEQ],
                                        ALU.subtract).then_inc(xm_lo, 1)

            def norm_start():
                norm.add()
                wait(dve, (msq_summed, norm.now))
                nc.vector.memset(square_sum[:, :, :], 0.0)
                nc.vector.tensor_scalar(mean_sq[:, :], msq_ps, NORM_EPS, None, ALU.add).then_inc(msq_ready, 1)

            def refine(result, start, square):
                t = newton[:, 0:square.shape[1]]
                own(nc.vector.scalar_tensor_tensor(out=t, in0=start, scalar=-0.5, in1=start, op0=ALU.mult,
                                                   op1=ALU.mult))
                own(nc.vector.tensor_tensor(t, t, square, ALU.mult))
                own(nc.vector.scalar_tensor_tensor(out=result, in0=t, scalar=1.5, in1=start, op0=ALU.add,
                                                   op1=ALU.mult))

            def norm_rstd():
                wait(dve, (inv_ready, norm.now))
                refine(rstd[:, :], inv[:, :], mean_sq[:, :])

            def scaled(target, by):
                summed = sum_acc()
                return nc.vector.tensor_tensor(target, summed, wide(by[:, :]), ALU.mult)

            def ffn(g_next, new_layer=None):
                def gate_up(i, first):
                    lo()
                    lo()
                    if first:
                        norm_start()
                        lo()
                    gate = sum_acc()
                    if first:
                        norm_rstd()
                        nc.vector.tensor_scalar(half_rstd[:, :], rstd[:, :], 0.5, None, ALU.mult)
                    nc.vector.tensor_tensor(gate, gate, wide(rstd[:, :]), ALU.mult).then_inc(gate_ready, 1)
                    lo()
                    if not first:
                        lo()
                    hidden.add()
                    h_at = hm[:, at(i * PAIR), :]
                    if not first:
                        for ap in (h_at[:, :, 0:SEQ], h_at[:, :, SEQ:2 * SEQ]):
                            dve.lower_ap(ap)
                    up = sum_acc()
                    wait(dve, (silu_done, hidden.now))
                    nc.vector.tensor_tensor(hid[:, :, :], up, silu[:, :, :],
                                            ALU.mult).then_inc(hid_ready, 1)
                    wait(dve, (hid_hi, hidden.now))
                    nc.vector.tensor_tensor(h_at[:, :, SEQ:2 * SEQ], hid[:, :, :], h_at[:, :, 0:SEQ],
                                            ALU.subtract).then_inc(hid_lo, 1)

                gate_up(0, True)
                with loop(dve, GU_ITERS, {split: 4, sets: 2, copies: 2, hidden: 1, step: 0}, 1) as i:
                    gate_up(i, False)
                if new_layer is not None:
                    par_at = pars[:, bass.ds(new_layer, 1), :].rearrange("p o n -> p (o n)")
                    dve.wait_ge(pars_ready, DEPTH)
                    nc.vector.tensor_copy(cur[:, :], par_at)
                with loop(dve, DOWN_ITERS, {split: 12, sets: 2, copies: 2, pair: 2, step: 2}) as i:
                    for j in range(2):
                        for k in range(DOWN_UNITS):
                            u = k + LEAD
                            lo(FT - UK * (DOWN_UNITS - 1) if u == DOWN_UNITS - 1 else UK)
                        t = i * (2 * PAIR) + j * PAIR
                        x_at = xt[:, at(t), :]
                        dve.lower_ap(x_at)
                        summed = sum_acc()
                        own(nc.vector.tensor_tensor(summed, summed, wide(half_rstd[:, :]),
                                                    ALU.mult))
                        nc.vector.tensor_tensor(x_at, x_at, summed, ALU.add).then_inc(x_new, 1)
                        moving_x(t, cur[:, bass.ds(i * (2 * PAIR) + (g_next + j * PAIR), PAIR)])

            dve.sem_inc(used, RING)
            dve.sem_inc(lo_split, RING)
            dve.sem_inc(acc_summed, ACCS)
            dve.sem_inc(pv_read, 1)
            dve.sem_inc(square_added, 1)
            dve.wait_ge(gain_loaded, 16)
            for first in range(0, XPAIRS, 2):
                for p in (first, first + 1):
                    dve.wait_ge(x_new, p + 1)
                    nc.vector.tensor_tensor(
                        xg[:, at(p * PAIR), :], xt[:, at(p * PAIR), :],
                        first_g[:, at(p * PAIR)].unsqueeze(2).to_broadcast([P, PAIR, SEQ]),
                        ALU.mult).then_inc(xg_ready, 1)
                if first:
                    lo()
                else:
                    dve.wait_ge(table_loaded, 32)
                    table_at = table[0:NUM_BUCKETS, :].unsqueeze(2).to_broadcast([NUM_BUCKETS, N_HEADS, P])
                    own(nc.vector.tensor_copy(table_hi[0:NUM_BUCKETS, :, :], table_at))
                    nc.vector.tensor_tensor(table_lo[0:NUM_BUCKETS, :, :], table_at, table_hi[0:NUM_BUCKETS, :, :],
                                        ALU.subtract).then_inc(table_ready, 1)
                for p in (first, first + 1):
                    dve.wait_ge(xm_hi, p + 1)
                    nc.vector.tensor_tensor(xm[:, at(p * PAIR), SEQ:2 * SEQ], xg[:, at(p * PAIR), :],
                                            xm[:, at(p * PAIR), 0:SEQ], ALU.subtract).then_inc(xm_lo, 1)
                lo()
            for p, more in enumerate((square, acc_lo[0], acc_lo[1]), 1):
                dve.wait_ge(squared, p + 1)
                dve.wait_ge(square_added, p)
                nc.vector.tensor_tensor(square_sum[:, :, :], square_sum[:, :, :], more[:, :, :],
                                        ALU.add).then_inc(square_added, 1)
            pair.add(XPAIRS)
            with loop(dve, DEPTH, {split: UNITS_LAYER, sets: SETS_LAYER, copies: COPIES_LAYER,
                                   pair: 3 * XPAIRS, norm: NORMS_LAYER, hidden: 2 * GU_ITERS, head: N_HEADS, layers: 1, branch_pairs: XPAIRS,
                                   gated: 2 * BRANCH_ITERS, step: STEPS_LAYER}) as l:
                ffn(P_MIX, l)
                def two_pairs(i, first):
                    lo()
                    lo()
                    if first:
                        norm_start()
                        lo()
                    for j in range(2):
                        p_at = proj[:, at(i * (2 * PAIR) + j * PAIR), :]
                        if not first:
                            dve.lower_ap(p_at)
                        summed = sum_acc()
                        if first and j == 0:
                            norm_rstd()
                        nc.vector.tensor_tensor(p_at, summed, wide(rstd[:, :]), ALU.mult).then_inc(proj_ready, 1)
                        if j == 0:
                            lo()
                            if not first:
                                lo()

                two_pairs(0, True)
                with loop(dve, QKV_ITERS, {split: 4, sets: 2, copies: 2}, 1) as i:
                    two_pairs(i, False)
                dve.wait_ge(bias_loaded, 32)
                with loop(dve, HEAD_ITERS, {split: 4, sets: 2, copies: 2, head: 1, step: HEAD_STEPS}) as h:
                    head.add()
                    b_at = bias[:, bass.ds(h, 1), :].to_broadcast([P, 2, KEYS])
                    dve.lower_ap(b_at)
                    wait(dve, (scored, head.now))
                    own(nc.vector.scalar_tensor_tensor(out=logits[:, :, :], in0=score[:, :, 0:KEYS],
                                                       scalar=HEAD_DIM ** -0.5, in1=b_at, op0=ALU.mult,
                                                       op1=ALU.add))
                    nc.vector.tensor_reduce(row_max[:, 1, :], logits[:, :, 0:SEQ], AX.X, ALU.max)
                    own(nc.vector.tensor_reduce(row_max[:, 0, :], logits[:, :, SEQ:], AX.X, ALU.max))
                    nc.vector.tensor_scalar(neg_max[:, :, :], row_max[:, :, :], -1.0, None,
                                            ALU.mult).then_inc(max_ready, 1)
                    lo()
                    lo()
                    wait(dve, (exp_done, head.now))
                    own(nc.vector.reciprocal(row_inv[:, :, :], row_sum[:, :, :]))
                    own(nc.vector.tensor_scalar(lam_inv[:, :], row_inv[:, :, 1], cur[:, P_LAM:P_LAM + 1], None,
                                                ALU.mult))
                    for t, (a, b) in enumerate(((SEQ, KEYS), (0, SEQ))):
                        own(nc.vector.tensor_scalar(expo[:, 1, a:b], expo[:, 1, a:b], lam_inv[:, t:t + 1], None,
                                                    ALU.mult))
                        last = nc.vector.scalar_tensor_tensor(
                            out=prob[:, a:b], in0=expo[:, 0, a:b], scalar=row_inv[:, t, 0:1], in1=expo[:, 1, a:b],
                            op0=ALU.mult, op1=ALU.subtract)
                    last.then_inc(prob_ready, 1)
                    for j in range(2):
                        l_at = late[:, bass.ds(h * (2 * PAIR) + j * PAIR, PAIR), :]
                        dve.lower_ap(l_at)
                        scaled(l_at, rstd)
                        if j == 0:
                            lo()
                            lo()
                layers.add()
                def gate_pair(i, j):
                    t = (HEAD_ITERS + i) * 2 * PAIR + j * PAIR
                    scaled(late[:, t:t + PAIR, :], rstd)

                def taps(k):
                    d = CONV_K - 1 - k
                    for t in range(CONV_T):
                        tap = P_CONV + k * CONV_T + t
                        last = nc.vector.scalar_tensor_tensor(
                            out=conv[:, t, d:], in0=conv_in[:, t, 0:SEQ - d], scalar=cur[:, tap:tap + 1],
                            in1=conv[:, t, d:], op0=ALU.mult, op1=ALU.add)
                    own(last)

                lo()
                nc.vector.tensor_tensor(conv_in, conv_in, conv, ALU.mult).then_inc(conv_in_ready, 1)
                lo()
                gate_pair(0, 0)
                wait(dve, (attn_squared, layers.now))
                nc.vector.tensor_scalar(attn_ms[:, :], attn_sq[:, :], 1.0 / V_DIM, SUBLN_EPS,
                                        ALU.mult, ALU.add).then_inc(attn_ms_ready, 1)
                lo()
                lo()
                gate_pair(0, 1)
                lo()
                wait(dve, (attn_inv_ready, layers.now))
                refine(attn_rstd[:, :], attn_inv[:, :], attn_ms[:, :])
                dve.sem_inc(attn_rstd_ready, 1)
                lo()
                gate_pair(1, 0)
                wait(dve, (conv_started, layers.now))
                taps(0)
                lo()
                taps(1)
                lo()
                gate_pair(1, 1)
                nc.vector.tensor_tensor(conv, conv, conv_b, ALU.mult).then_inc(conv_ready, 1)
                lo()
                lo()
                gate_pair(2, 0)
                wait(dve, (attn_hi, layers.now))
                nc.vector.tensor_tensor(mix[:, 0:N_HEADS, SEQ:2 * SEQ],
                                        attn[:, :, :, :].rearrange("p h t d -> p h (t d)"),
                                        mix[:, 0:N_HEADS, 0:SEQ], ALU.subtract).then_inc(mix_lo, 1)
                lo()
                lo()
                wait(dve, (conv_hi, layers.now))
                nc.vector.tensor_tensor(mix[:, N_HEADS:, SEQ:2 * SEQ], conv, mix[:, N_HEADS:, 0:SEQ],
                                        ALU.subtract).then_inc(mix_lo, 1)
                gate_pair(2, 1)
                with loop(dve, BRANCH_ITERS, {split: 4, sets: 4, branch_pairs: 2, gated: 2}) as i:
                    before = split.now - LEAD + RING
                    for g in range(2):
                        gated.add()
                        for j in range(2):
                            lo()
                            n = 2 * g + j
                            g_at = gates[:, bass.ds(i * (2 * PAIR) + (g * KT + j * PAIR), PAIR), :]
                            p_at = part[:, j * PAIR:(j + 1) * PAIR, :]
                            dve.lower_ap(g_at)
                            if j == 0:
                                wait(dve, (gates_done, gated.now))
                            if g == 0:
                                wait(dve, (lo_split, split.now + RING))
                                take(p_at, merge_sets[n], g_at, ALU.mult, before + (n + 1))
                            else:
                                take(sums[j][:, :, :], merge_sets[n], g_at, ALU.mult, before + (n + 1))
                                taken()
                                nc.vector.tensor_tensor(p_at, p_at, sums[j][:, :, :],
                                                        ALU.add).then_inc(merged_ready, 1)
                    for j in range(2):
                        branch_pairs.add()
                        m_at = merged[:, bass.ds(i * (2 * PAIR) + j * PAIR, PAIR), :]
                        for ap in (m_at[:, :, 0:SEQ], m_at[:, :, SEQ:2 * SEQ]):
                            dve.lower_ap(ap)
                        wait(dve, (merged_hi, branch_pairs.now))
                        nc.vector.tensor_tensor(m_at[:, :, SEQ:2 * SEQ], part[:, j * PAIR:(j + 1) * PAIR, :],
                                                m_at[:, :, 0:SEQ], ALU.subtract).then_inc(merged_lo, 1)
                for i in range(OUT_ITERS):
                    before = split.now - LEAD + RING
                    for j in range(2):
                        for _ in range(2 if i else 3 - 2 * j):
                            lo()
                        t = (2 * i + j) * PAIR
                        x_at = xt[:, at(t), :]
                        take(x_at, acc[sets.fixed % ACCS], x_at, ALU.add,
                             before + (2 * (j + 1) if i else 3 + j))
                        taken()
                        dve.sem_inc(x_new, 1)
                        moving_x(t, cur[:, P_FFN2 + t:P_FFN2 + t + PAIR])
                ffn(P_NEXT)
            wait(dve, (msq_summed, norm.now + 1))
            nc.vector.tensor_scalar(out_ms[:, :], out_msq_ps, NORM_EPS, None, ALU.add).then_inc(msq_ready, 1)
            wait(dve, (inv_ready, norm.now + 1))
            refine(out_rstd[:, :], out_inv[:, :], out_ms[:, :])
            dve.sem_inc(out_rstd_ready, 1)
            for b in range(2, XPAIRS):
                dve.wait_ge(y_turned, b + 1)
                for t in range(QT):
                    last = nc.vector.tensor_scalar(y_at(b, t), turned_at(b, t), out_rstd[:, t:t + 1], None, ALU.mult)
                last.then_inc(y_copied[1], 1)

        @block.tensor
        def _(pe):
            unit = Count()
            sets = Count()
            norm = Count()
            pairs = Count()
            hidden = Count()
            head = Count()
            layers = Count()
            mixes = Count()
            branch_pairs = Count()
            slot = [0]

            def multiply(banks, x_tiles, first, last, *needs, halves=True):
                r = slot[0] % RING
                wait(pe, *needs, (hi_split, unit.now + 1), (lo_split, unit.now + 1 + RING))
                for k, x in enumerate(x_tiles):
                    for m in range(PAIR):
                        cols = slice(m * P, (m + 1) * P)
                        end = last and k == len(x_tiles) - 1
                        if halves:
                            nc.tensor.matmul(banks[:, m, :], w_hi[:, r, k, cols], x[:, 0:2 * SEQ],
                                             start=first and k == 0, stop=False, skip_group_check=True)
                        else:
                            for at_x in (0, SEQ):
                                nc.tensor.matmul(banks[:, m, 0:SEQ], w_hi[:, r, k, cols], x[:, at_x:at_x + SEQ],
                                                 start=first and k == 0 and at_x == 0, stop=False,
                                                 skip_group_check=True)
                        mm = nc.tensor.matmul(banks[:, m, 0:SEQ], w_lo[:, r, k, cols], x[:, 0:SEQ],
                                              start=False, stop=end, skip_group_check=True)
                mm.then_inc(used, 1)
                unit.add()
                slot[0] += 1

            def new_set(banks=None, ahead=ACCS):
                banks = acc[sets.fixed % ACCS] if banks is None else banks
                sets.add()
                wait(pe, (acc_summed, sets.now + ACCS - ahead))
                return banks

            def two_sets(tiles, made, count, in_turn=False, between=None, halves=True):
                banks = [None, None]
                order = [(j, n) for n in range(2) for j in range(2)] if in_turn else \
                    [(j, n) for j in range(2) for n in range(2)]
                for j, n in order:
                    if n == 0:
                        banks[j] = new_set()
                    if between and (j, n) == (0, 1):
                        between()
                    multiply(banks[j], [tiles[:, n * UK + k, :] for k in range(UK)], n == 0, n == 1,
                             (made, count.now - (1 - n) * UK // PAIR), halves=halves)

            def mean_square():
                wait(pe, (square_added, pairs.now), (bias_copied, 1))
                for m in range(PAIR):
                    mm = nc.tensor.matmul(msq_ps, mean_ones[:, :], square_sum[:, m, :], start=(m == 0),
                                          stop=(m == PAIR - 1))
                mm.then_inc(msq_summed, 1)
                norm.add()

            def normed_sets(iterations):
                two_sets(xm, xm_lo, pairs, True, mean_square)
                with loop(pe, iterations, {unit: 4, sets: 2}, 1):
                    two_sets(xm, xm_lo, pairs)

            def ffn():
                normed_sets(GU_ITERS)
                hidden.add(GU_ITERS)
                with loop(pe, DOWN_ITERS, {unit: 12, sets: 2}):
                    for _ in range(2):
                        s = new_set()
                        for n in range(DOWN_UNITS):
                            tiles = range(n * UK, min((n + 1) * UK, FT))
                            multiply(s, [hm[:, k, :] for k in tiles], n == 0, n == DOWN_UNITS - 1,
                                     (hid_lo, hidden.now - (FT - 1 - tiles[-1]) // PAIR))
                pairs.add(XPAIRS)

            pe.wait_ge(ident_ready, 1)
            for b in range(XPAIRS):
                pe.wait_ge(x_loaded[b // 2], 16)
                for k in range(2):
                    for t in range(QT):
                        col = (k * QT + t) * P
                        kt = 2 * b + k
                        mm = nc.tensor.transpose(acc[b // 2][:, b % 2, col:col + P],
                                                 x_tok[:, t, kt * P:(kt + 1) * P], ident[:, :])
                mm.then_inc(x_turned, 1)
            pairs.add(XPAIRS)
            pe.wait_ge(table_ready, 1)
            pe.wait_ge(onehot_ready, 1)
            for h in range(N_HEADS):
                for n, part_of in enumerate((table_hi, table_lo)):
                    mm = nc.tensor.matmul(side[h][:, 0:BIAS_LEN], part_of[0:NUM_BUCKETS, h, :],
                                          onehot_r[0:NUM_BUCKETS, :], start=n == 0, stop=n == 1)
            mm.then_inc(bias_spread, 1)
            pe.wait_ge(x_new, XPAIRS)
            with loop(pe, DEPTH, {unit: UNITS_LAYER, sets: SETS_LAYER, norm: NORMS_LAYER, pairs: 3 * XPAIRS,
                                  hidden: 2 * GU_ITERS, head: N_HEADS, layers: 1,
                                  branch_pairs: XPAIRS, mixes: 2}):
                ffn()
                normed_sets(QKV_ITERS)

                def first_unit():
                    multiply(new_set(), [xm[:, k, :] for k in range(UK)], True, False)

                def other_units():
                    multiply(acc[(sets.fixed - 1) % ACCS], [xm[:, k, :] for k in range(UK, KT)], False, True)
                    first_unit()
                    multiply(acc[(sets.fixed - 1) % ACCS], [xm[:, k, :] for k in range(UK, KT)], False, True)

                first_unit()
                with loop(pe, HEAD_ITERS, {unit: 4, sets: 2, head: 1}):
                    head.add()
                    wait(pe, (head_copied, head.now + layers.now))
                    for sm in range(2):
                        half = slice(sm * HEAD_DIM, (sm + 1) * HEAD_DIM)
                        nc.tensor.matmul(score[:, sm, 0:SEQ], head_qkv[half, 0, P:SEQ], head_qkv[half, 1, :],
                                         start=True, stop=True)
                        mm = nc.tensor.matmul(score[:, sm, SEQ:KEYS], head_qkv[half, 0, 0:P],
                                              head_qkv[half, 1, 0:P], start=True, stop=True)
                    mm.then_inc(scored, 1)
                    wait(pe, (pv_read, head.now))
                    for t in range(QT):
                        mm = nc.tensor.transpose(v_ps[:, t * V_DIM:(t + 1) * V_DIM],
                                                 head_qkv[:, 2, t * P:(t + 1) * P], ident[:, :])
                    mm.then_inc(v_turned, 1)
                    other_units()
                    wait(pe, (prob_ready, head.now))
                    for b in range(KEYS // P):
                        mm = nc.tensor.transpose(prob_t_ps[:, b * P:(b + 1) * P], prob[:, b * P:(b + 1) * P],
                                                 ident[:, :])
                    mm.then_inc(prob_turned, 1)
                    first_unit()
                    wait(pe, (v_copied, head.now), (prob_copied, head.now))
                    for k in range(QT):
                        nc.tensor.matmul(pv_ps[:, 1, :], prob_t[:, k * P:(k + 1) * P], v_tok[:, k, :],
                                         start=(k == 0), stop=(k == QT - 1))
                    nc.tensor.matmul(pv_ps[:, 0, :], prob_t[:, SEQ:KEYS], v_tok[:, 0, :], start=True,
                                     stop=True).then_inc(pv_done, 1)
                with loop(pe, GATE_ITERS - 1, {unit: 4, sets: 2}):
                    other_units()
                    first_unit()
                layers.add()
                wait(pe, (attn_scaled, layers.now))
                for h in range(N_HEADS):
                    for t in range(QT):
                        col = ((h % 2) * QT + t) * P
                        mm = nc.tensor.transpose(side[h // 2][:, col:col + P], attn[:, h, t, :], ident[:, :])
                mm.then_inc(attn_turned, 1)
                other_units()
                mixes.add(2)
                with loop(pe, BRANCH_ITERS, {unit: 4, sets: 4}):
                    for n in range(2):
                        for j in range(2):
                            multiply(new_set(merge_sets[2 * n + j], len(merge_sets)),
                                     [mix[:, n * UK + k, :] for k in range(UK)], True, True,
                                     (mix_lo, mixes.now - 1 + n), halves=False)
                branch_pairs.add(XPAIRS)
                for i in range(OUT_ITERS):
                    two_sets(merged, merged_lo, branch_pairs, in_turn=i == 0, halves=False)
                pairs.add(XPAIRS)
                ffn()
            for b in range(XPAIRS):
                pe.wait_ge(xg_ready, pairs.now - (XPAIRS - 1 - b))
                for k in range(2):
                    for t in range(QT):
                        col = (k * QT + t) * P
                        mm = nc.tensor.transpose(side[b][:, col:col + P], xg[:, 2 * b + k, t * P:(t + 1) * P],
                                                 ident[:, :])
                mm.then_inc(y_turned, 1)
            wait(pe, (square_added, pairs.now))
            for t in range(QT):
                for m in range(PAIR):
                    mm = nc.tensor.matmul(out_msq_ps[:, t:t + 1], square_sum[:, m, t * P:(t + 1) * P],
                                          mean_ones[:, 0:1], start=(m == 0), stop=(m == PAIR - 1))
            mm.then_inc(msq_summed, 1)


_INS = ["x", "norm_ffn1_g", "ffn1_w_gate", "ffn1_w_up", "ffn1_w_down", "norm_mix_g", "w_in", "lambda_q1",
        "lambda_k1", "lambda_q2", "lambda_k2", "subln_g", "rel_bias", "conv_w", "w_branch_attn",
        "w_branch_conv", "w_out", "norm_ffn2_g", "ffn2_w_gate", "ffn2_w_up", "ffn2_w_down", "final_g"]


def kernel(**inputs):
    import numpy as _np
    import concourse.bacc as _bacc
    from concourse import mybir as _mybir
    from concourse.bass_utils import run_bass_kernel_spmd as _run

    nc = _bacc.Bacc("TRN2", target_bir_lowering=False, num_devices=1)
    arrays, args = {}, []
    for name in _INS + ["places"]:
        a = bucket_places() if name == "places" else _np.ascontiguousarray(inputs[name])
        arrays[f"in_{name}_dram"] = a
        args.append(nc.dram_tensor(f"in_{name}_dram", a.shape, _mybir.dt.from_np(a.dtype), kind="ExternalInput").ap())
    out = nc.dram_tensor("out_0_dram", (1, SEQ, D_MODEL), F32, kind="ExternalOutput").ap()
    trunk(nc, *args, out)
    r = _run(nc, [arrays], core_ids=[0])
    return r.results[0]["out_0_dram"]
```
